# Optimizing a Trainium2 kernel written in Bass

```python
import math
import jax, jax.numpy as jnp
from jax import lax
import numpy as np

D_MODEL = 1024
BATCH = 1
SEQ = 256
DEPTH = 2

BRANCH_WIDTH = 512
N_BRANCHES = 3
HEAD_DIM = 64
NSA_HEADS = BRANCH_WIDTH // HEAD_DIM
NSA_KV_GROUPS = 2
NSA_GROUP = NSA_HEADS // NSA_KV_GROUPS
NSA_WIDTH = NSA_HEADS * HEAD_DIM
CMP_LEN = 32
CMP_STRIDE = 16
SLC_BLOCK = 64
SLC_TOPN = 16
WINDOW = 512
CMP_HIDDEN = 256
Q_BLOCK = 128
CONV_WIDTH = BRANCH_WIDTH
CONV_K = 3
RET_HEADS = 4
RET_HEAD_DIM = BRANCH_WIDTH // RET_HEADS
RET_WIDTH = RET_HEADS * RET_HEAD_DIM
RET_CHUNK = 128
ROPE_BASE = 10000.0
D_FF = 3584
N_EXPERTS = 8
TOP_K = 2
N_DENSE = (DEPTH + 1) // 2
N_MOE = DEPTH // 2
LN_EPS = 1e-5
ALPHA = (2.0 * DEPTH) ** 0.25
BETA = (8.0 * DEPTH) ** -0.25
SPLIT_SIZES = (NSA_WIDTH, 6 * NSA_KV_GROUPS * HEAD_DIM, 3 * NSA_HEADS,
               CONV_WIDTH, CONV_WIDTH, CONV_WIDTH,
               RET_WIDTH, RET_WIDTH, RET_WIDTH, RET_WIDTH,
               N_BRANCHES * D_MODEL)
IN_COLS = sum(SPLIT_SIZES)

kernel_name = "hybrid_nsa_conv_retention_moe_deepnorm"

def split_points():
    pts, acc = [], 0
    for s in SPLIT_SIZES[:-1]:
        acc += s
        pts.append(acc)
    return pts

def layer_norm(x, g, b):
    xf = x.astype(jnp.float32)
    mu = xf.mean(-1, keepdims=True)
    var = jnp.square(xf - mu).mean(-1, keepdims=True)
    return ((xf - mu) * lax.rsqrt(var + LN_EPS)).astype(x.dtype) * g + b

def masked_softmax(s, mask):
    s = jnp.where(mask, s.astype(jnp.float32), -jnp.inf)
    m = jnp.max(s, axis=-1, keepdims=True)
    m = jnp.where(jnp.isfinite(m), m, 0.0)
    p = jnp.exp(s - m)
    return p / jnp.maximum(p.sum(-1, keepdims=True), 1e-30)

def nsa_compress(kv, pos, w1, b1, w2, b2):
    b, t, g, dh = kv.shape
    chunks = kv.reshape(b, t // CMP_STRIDE, CMP_STRIDE, g, dh)
    blocks = jnp.concatenate([chunks[:, :-1], chunks[:, 1:]], axis=2) + pos[:, None, :]
    nc = blocks.shape[1]
    flat = blocks.transpose(0, 1, 3, 2, 4).reshape(b, nc, g, CMP_LEN * dh)
    hid = jax.nn.gelu(flat @ w1 + b1)
    return hid @ w2 + b2

def nsa_attention(q, k_cmp, v_cmp, k_slc, v_slc, k_win, v_win, gates):
    b, t, h, dh = q.shape
    G, R = NSA_KV_GROUPS, NSA_GROUP
    qg = q.reshape(b, t, G, R, dh).transpose(0, 2, 3, 1, 4) * (dh ** -0.5)
    kc = k_cmp.transpose(0, 2, 1, 3)
    vc = v_cmp.transpose(0, 2, 1, 3)
    nc = kc.shape[2]
    n_sel = t // SLC_BLOCK
    topn = min(SLC_TOPN, n_sel)
    ratio = SLC_BLOCK // CMP_STRIDE
    ks = k_slc.transpose(0, 2, 1, 3).reshape(b, G, n_sel, SLC_BLOCK, dh)
    vs = v_slc.transpose(0, 2, 1, 3).reshape(b, G, n_sel, SLC_BLOCK, dh)
    pad_w = ((0, 0), (0, 0), (WINDOW, 0), (0, 0))
    kw = jnp.pad(k_win.transpose(0, 2, 1, 3), pad_w)
    vw = jnp.pad(v_win.transpose(0, 2, 1, 3), pad_w)
    cmp_end = jnp.arange(nc) * CMP_STRIDE + CMP_LEN - 1
    right_pad = ratio * (n_sel + 1) - 1 - nc
    b_idx = jnp.arange(b)[:, None, None, None]
    g_idx = jnp.arange(G)[None, :, None, None]
    j_blk = jnp.arange(n_sel)

    def block_fn(qb):
        q0 = qb * Q_BLOCK
        tq = q0 + jnp.arange(Q_BLOCK)
        qq = lax.dynamic_slice_in_dim(qg, q0, Q_BLOCK, axis=3)
        s_c = jnp.einsum('bgrqd,bgnd->bgrqn', qq, kc)
        p_c = masked_softmax(s_c, cmp_end[None, :] <= tq[:, None])
        o_c = jnp.einsum('bgrqn,bgnd->bgrqd', p_c.astype(vc.dtype), vc)
        p_grp = p_c.sum(axis=2)
        p_pad = jnp.pad(p_grp, ((0, 0), (0, 0), (0, 0), (1, right_pad)))
        P = p_pad.reshape(b, G, Q_BLOCK, n_sel + 1, ratio)
        score = (P[..., :n_sel, 0] + 2.0 * (P[..., :n_sel, 1] + P[..., :n_sel, 2] + P[..., :n_sel, 3])
                 + P[..., 1:, 0])
        cur = tq // SLC_BLOCK
        valid = j_blk[None, :] <= cur[:, None]
        forced = (j_blk[None, :] == 0) | (j_blk[None, :] == cur[:, None]) | (j_blk[None, :] == cur[:, None] - 1)
        score = jnp.where(forced, 1e9, score)
        score = jnp.where(valid, score, -1.0)
        _, idx = lax.top_k(score, topn)
        k_sel = ks[b_idx, g_idx, idx]
        v_sel = vs[b_idx, g_idx, idx]
        s_s = jnp.einsum('bgrqd,bgqnkd->bgrqnk', qq, k_sel).reshape(b, G, R, Q_BLOCK, -1)
        kpos_s = idx[..., None] * SLC_BLOCK + jnp.arange(SLC_BLOCK)
        m_s = (kpos_s <= tq[None, None, :, None, None]).reshape(b, G, 1, Q_BLOCK, -1)
        p_s = masked_softmax(s_s, m_s).reshape(b, G, R, Q_BLOCK, topn, SLC_BLOCK)
        o_s = jnp.einsum('bgrqnk,bgqnkd->bgrqd', p_s.astype(v_sel.dtype), v_sel)
        kwb = lax.dynamic_slice_in_dim(kw, q0, Q_BLOCK + WINDOW, axis=2)
        vwb = lax.dynamic_slice_in_dim(vw, q0, Q_BLOCK + WINDOW, axis=2)
        kpos_w = q0 - WINDOW + jnp.arange(Q_BLOCK + WINDOW)
        m_w = ((kpos_w[None, :] <= tq[:, None]) & (kpos_w[None, :] > tq[:, None] - WINDOW)
               & (kpos_w[None, :] >= 0))
        s_w = jnp.einsum('bgrqd,bgkd->bgrqk', qq, kwb)
        p_w = masked_softmax(s_w, m_w)
        o_w = jnp.einsum('bgrqk,bgkd->bgrqd', p_w.astype(vwb.dtype), vwb)
        return o_c, o_s, o_w

    o_c, o_s, o_w = lax.map(block_fn, jnp.arange(t // Q_BLOCK))

    def to_bthd(o):
        return o.transpose(1, 0, 4, 2, 3, 5).reshape(b, t, h, dh)

    y = gates[..., 0:1] * to_bthd(o_c) + gates[..., 1:2] * to_bthd(o_s) + gates[..., 2:3] * to_bthd(o_w)
    return y.reshape(b, t, h * dh)

def short_conv(bx, cx, hx, w_conv):
    u = cx * hx
    y = lax.conv_general_dilated(u, w_conv[:, None, :], window_strides=(1,), padding=((CONV_K - 1, 0),),
                                 dimension_numbers=('NWC', 'WIO', 'NWC'), feature_group_count=CONV_WIDTH)
    return bx * y

def rotary(x, pos):
    d = x.shape[-1]
    inv = ROPE_BASE ** (-jnp.arange(0, d, 2, dtype=jnp.float32) / d)
    ang = pos.astype(jnp.float32)[:, None] * inv[None, :]
    cos = jnp.cos(ang)[None, :, None, :].astype(x.dtype)
    sin = jnp.sin(ang)[None, :, None, :].astype(x.dtype)
    x1, x2 = x[..., : d // 2], x[..., d // 2:]
    return jnp.concatenate([x1 * cos - x2 * sin, x1 * sin + x2 * cos], axis=-1)

def retention(q, k, v):
    b, t, h, d = q.shape
    C = RET_CHUNK
    n = t // C
    log_g = jnp.log(1.0 - 2.0 ** (-5.0 - jnp.arange(h, dtype=jnp.float32)))
    idx = jnp.arange(C, dtype=jnp.float32)
    diff = idx[:, None] - idx[None, :]
    decay_in = jnp.where(diff >= 0, jnp.exp(log_g[:, None, None] * jnp.maximum(diff, 0.0)), 0.0)
    q_dec = jnp.exp(log_g[:, None] * (idx + 1.0))[None, :, :, None]
    k_dec = jnp.exp(log_g[:, None] * (C - 1.0 - idx))[None, :, :, None]
    chunk_dec = jnp.exp(log_g * C)[None, :, None, None]

    def chunks(a):
        return a.astype(jnp.float32).reshape(b, n, C, h, d).transpose(1, 0, 3, 2, 4)

    def step(state, inp):
        qi, ki, vi = inp
        inner = jnp.einsum('bhqd,bhkd->bhqk', qi, ki) * decay_in
        o = jnp.einsum('bhqk,bhkd->bhqd', inner, vi) + jnp.einsum('bhqd,bhde->bhqe', qi, state) * q_dec
        state = state * chunk_dec + jnp.einsum('bhkd,bhke->bhde', ki * k_dec, vi)
        return state, o

    state0 = jnp.zeros((b, h, d, d), jnp.float32)
    _, o = lax.scan(step, state0, (chunks(q), chunks(k), chunks(v)))
    return o.transpose(1, 0, 3, 2, 4).reshape(b, t, h, d).astype(q.dtype)

def group_norm(o, g, bias):
    of = o.astype(jnp.float32)
    mu = of.mean(-1, keepdims=True)
    var = jnp.square(of - mu).mean(-1, keepdims=True)
    y = ((of - mu) * lax.rsqrt(var + LN_EPS)).astype(o.dtype)
    return y.reshape(o.shape[0], o.shape[1], -1) * g + bias

def token_mixer(x, w_in, cmp_pos, cmp_w1, cmp_b1, cmp_w2, cmp_b2, conv_w, gn_g, gn_b, w_br, w_out):
    b, t, _ = x.shape
    hcat = x @ w_in
    (q, kv, ngate, cb, cc, ch, rq, rk, rv, rg, mgate) = jnp.split(hcat, split_points(), axis=-1)
    q = q.reshape(b, t, NSA_HEADS, HEAD_DIM)
    kv = kv.reshape(b, t, 3, 2, NSA_KV_GROUPS, HEAD_DIM)
    k_cmp = nsa_compress(kv[:, :, 0, 0], cmp_pos[0], cmp_w1[0], cmp_b1[0], cmp_w2[0], cmp_b2[0])
    v_cmp = nsa_compress(kv[:, :, 0, 1], cmp_pos[1], cmp_w1[1], cmp_b1[1], cmp_w2[1], cmp_b2[1])
    nsa_g = jax.nn.sigmoid(ngate).reshape(b, t, NSA_HEADS, 3)
    y_a = nsa_attention(q, k_cmp, v_cmp, kv[:, :, 1, 0], kv[:, :, 1, 1], kv[:, :, 2, 0], kv[:, :, 2, 1], nsa_g)
    y_b = short_conv(cb, cc, ch, conv_w)
    pos = jnp.arange(t)
    rq = rotary(rq.reshape(b, t, RET_HEADS, RET_HEAD_DIM), pos)
    rk = rotary(rk.reshape(b, t, RET_HEADS, RET_HEAD_DIM), pos) * (RET_HEAD_DIM ** -0.5)
    o_r = retention(rq, rk, rv.reshape(b, t, RET_HEADS, RET_HEAD_DIM))
    y_c = jax.nn.silu(rg) * group_norm(o_r, gn_g, gn_b)
    ys = jnp.stack([y_a, y_b, y_c], axis=2)
    proj = jnp.einsum('btcw,cwd->btcd', ys, w_br)
    gates = jax.nn.sigmoid(mgate).reshape(b, t, N_BRANCHES, D_MODEL)
    return jnp.sum(gates * proj, axis=2) @ w_out

def swiglu(x, w_gate, w_up, w_down):
    return (jax.nn.silu(x @ w_gate) * (x @ w_up)) @ w_down

def moe_swiglu(x, w_router, w_gate, w_up, w_down):
    logits = (x @ w_router).astype(jnp.float32)
    top_v, top_i = lax.top_k(logits, TOP_K)
    probs = jax.nn.softmax(top_v, axis=-1)
    combine = jnp.sum(jax.nn.one_hot(top_i, N_EXPERTS, dtype=jnp.float32) * probs[..., None], axis=-2)
    combine = combine.astype(x.dtype)
    out = jnp.zeros_like(x)
    for e in range(N_EXPERTS):
        out = out + combine[..., e:e + 1] * swiglu(x, w_gate[e], w_up[e], w_down[e])
    return out

def setup_inputs(seed: int = 0) -> dict:
    key = jax.random.key(seed)
    ks = jax.random.split(key, 24)
    f32 = jnp.float32

    def nrm(k, shape, scale):
        return jax.random.normal(k, shape, f32) * scale

    L = DEPTH
    return {
        "x": nrm(ks[0], (BATCH, SEQ, D_MODEL), 1.0),
        "w_in": nrm(ks[1], (L, D_MODEL, IN_COLS), D_MODEL ** -0.5),
        "cmp_pos": nrm(ks[2], (L, 2, CMP_LEN, HEAD_DIM), 0.1),
        "cmp_w1": nrm(ks[3], (L, 2, CMP_LEN * HEAD_DIM, CMP_HIDDEN), (CMP_LEN * HEAD_DIM) ** -0.5),
        "cmp_b1": nrm(ks[4], (L, 2, CMP_HIDDEN), 0.01),
        "cmp_w2": nrm(ks[5], (L, 2, CMP_HIDDEN, HEAD_DIM), CMP_HIDDEN ** -0.5),
        "cmp_b2": nrm(ks[6], (L, 2, HEAD_DIM), 0.01),
        "conv_w": nrm(ks[7], (L, CONV_K, CONV_WIDTH), CONV_K ** -0.5),
        "ret_gn_g": 1.0 + nrm(ks[8], (L, RET_WIDTH), 0.01),
        "ret_gn_b": nrm(ks[9], (L, RET_WIDTH), 0.01),
        "w_br": nrm(ks[10], (L, N_BRANCHES, BRANCH_WIDTH, D_MODEL), BETA * BRANCH_WIDTH ** -0.5),
        "w_out": nrm(ks[11], (L, D_MODEL, D_MODEL), BETA * D_MODEL ** -0.5),
        "ln1_g": 1.0 + nrm(ks[12], (L, D_MODEL), 0.01),
        "ln1_b": nrm(ks[13], (L, D_MODEL), 0.01),
        "ln2_g": 1.0 + nrm(ks[14], (L, D_MODEL), 0.01),
        "ln2_b": nrm(ks[15], (L, D_MODEL), 0.01),
        "ffn_gate": nrm(ks[16], (N_DENSE, D_MODEL, D_FF), D_MODEL ** -0.5),
        "ffn_up": nrm(ks[17], (N_DENSE, D_MODEL, D_FF), D_MODEL ** -0.5),
        "ffn_down": nrm(ks[18], (N_DENSE, D_FF, D_MODEL), BETA * D_FF ** -0.5),
        "moe_router": nrm(ks[19], (N_MOE, D_MODEL, N_EXPERTS), D_MODEL ** -0.5),
        "moe_gate": nrm(ks[20], (N_MOE, N_EXPERTS, D_MODEL, D_FF), D_MODEL ** -0.5),
        "moe_up": nrm(ks[21], (N_MOE, N_EXPERTS, D_MODEL, D_FF), D_MODEL ** -0.5),
        "moe_down": nrm(ks[22], (N_MOE, N_EXPERTS, D_FF, D_MODEL), BETA * D_FF ** -0.5),
    }

def reference(x, w_in, cmp_pos, cmp_w1, cmp_b1, cmp_w2, cmp_b2, conv_w, ret_gn_g, ret_gn_b, w_br, w_out,
              ln1_g, ln1_b, ln2_g, ln2_b, ffn_gate, ffn_up, ffn_down, moe_router, moe_gate, moe_up, moe_down):
    for l in range(DEPTH):
        m = token_mixer(x, w_in[l], cmp_pos[l], cmp_w1[l], cmp_b1[l], cmp_w2[l], cmp_b2[l], conv_w[l],
                        ret_gn_g[l], ret_gn_b[l], w_br[l], w_out[l])
        x = layer_norm(ALPHA * x + m, ln1_g[l], ln1_b[l])
        if l % 2 == 0:
            f = swiglu(x, ffn_gate[l // 2], ffn_up[l // 2], ffn_down[l // 2])
        else:
            f = moe_swiglu(x, moe_router[l // 2], moe_gate[l // 2], moe_up[l // 2], moe_down[l // 2])
        x = layer_norm(ALPHA * x + f, ln2_g[l], ln2_b[l])
    return x


_drawn_inputs = setup_inputs


def setup_inputs(seed=0):
    import zlib

    import numpy as np

    out = dict(_drawn_inputs(seed))
    spreads = {}
    factors = {'cmp_pos': 8.0,
     'cmp_b1': 41.564,
     'cmp_b2': 37.054,
     'ret_gn_g': 34.754,
     'ret_gn_b': 33.178,
     'ln1_g': 2.925,
     'ln2_g': 3.163,
     'ln2_b': 2.989,
     'ln1_b': 4.248}
    for name, (base, spread) in spreads.items():
        noise = np.random.default_rng([zlib.crc32(name.encode()), seed]).standard_normal(out[name].shape)
        drawn = base * np.exp(spread * noise) if base else spread * noise
        out[name] = __import__('jax').numpy.asarray(drawn.astype(out[name].dtype))
    for name, factor in factors.items():
        out[name] = (out[name] * factor).astype(out[name].dtype)
    return out
```

```python
from contextlib import ExitStack

import numpy as np

import concourse.bass as bass
from concourse import mybir

F32 = mybir.dt.float32
F32R = mybir.dt.float32r
BF16 = mybir.dt.bfloat16
I32 = mybir.dt.int32
U32 = mybir.dt.uint32
ALU = mybir.AluOpType
ACT = mybir.ActivationFunctionType
AX_X = mybir.AxisListType.X

P = 128
D = 1024
T = 256
TT = T // P
L = 2
DK = D // P
WB = 512
DH = 64
NH = WB // DH
NG = 2
NR = NH // NG
CL, CS = 32, 16
NC = T // CS - 1
CH = 256
RH = 4
RD = WB // RH
FF = 3584
NB = FF // 512
NE = 8
NX = (2 * T) // (P + 1)
NI = NE + NX
EPS = 1e-5
ALPHA = (2.0 * L) ** 0.25
NEG = -1e30
assert T // 64 <= 16 and T <= 512

SUB = 2048
MIX = 46
FFN = 6 * NB
LAYER = MIX + FFN
MOE0 = LAYER + MIX
RING = 3
NEXT = (0, MIX, LAYER, MOE0)
NTILES = (MOE0 + NE * FFN) // 2
ITEM_TILES = FFN // 2

PA = (0, 1)
SB = 2
TB = 4
YB = 6
MB = 7
ZM = 79
NORM_BANKS = (0, 1, 6, 7)
SCATTER = (MB, TB, TB + 1, YB)

UNITS = (["act"] * 2 + ["dve"] + ["act"] + ["dve"] + ["act"] + ["act"] * 2 + ["dve"] * 2 + ["dve"] * 2
         + ["dve"] * 4 + ["act"] * 2 + ["act"] * 2 + (["act"] * 2 + ["dve"] * 2) * 6)
NU = len(UNITS)
U_CONV_C, U_CONV_H, U_CONV_B, U_RQ, U_RK, U_RV, U_RG, U_BR = 6, 8, 10, 12, 14, 16, 18, 20

STEPS = []
for _qt in range(TT):
    STEPS += [("full", _qt, 0, 0), ("cmp", _qt, None, None), ("full", _qt, 0, 1), ("full", _qt, 1, 0),
              ("full", _qt, 1, 1)]
NS = len(STEPS)
STEP0 = 10
RET0 = STEP0 + 2 * NS + 1
GROUP_ENDS = [j for j, s in enumerate(STEPS) if s[0] == "full" and s[3] == 1]
BRANCH0 = 24
OUT0 = 42
FIRST_BRANCH, MID_BRANCH, LAST_BRANCH = 0, 1, 2

C_ID, C_DEC, C_COS, C_SIN, C_IOTA, C_IOTA8, C_TRI8, C_VALID = 0, 128, 1152, 1408, 1664, 1792, 1800, 1864
C_ONES = C_VALID + TT * NC
C_W = C_ONES + NC
B_ID, B_MASK, B_CMP, B_LT, B_ONE = 0, 128, 384, 384 + TT * NC, 512 + TT * NC
B_W = B_ONE + 128
S_POS, S_B1, S_W2K, S_W2V, S_B2K, S_CONV, S_GNG, S_GNB, S_B2V = 0, 256, 260, 516, 644, 645, 657, 661, 665
S_W = S_B2V + DH


def unit_count(u, who):
    return sum(w == who for w in UNITS[:u + 1])


def second_banks(j):
    return sum(k == "cmp" or qt == 1 for k, qt, _, _ in STEPS[:j + 1])


class Chain:

    def __init__(self, eng, sem):
        self.eng, self.sem, self.n = eng, sem, 0

    def mark(self, ins):
        ins.then_inc(self.sem, 1)
        self.n = self.n + 1

    def wait(self):
        self.eng.wait_ge(self.sem, self.n)

    def link(self, ins):
        self.mark(ins)
        self.wait()


def trunk(nc, wstream, x, consts, constb, small, ln, router, out):
    with ExitStack() as ctx:
        def sb(name, shape, dt=F32):
            return ctx.enter_context(nc.sbuf_tensor(name, shape, dt))

        def sem(name):
            return ctx.enter_context(nc.semaphore(name))

        raw = sb("raw", [P, RING, 2 * SUB])
        w_hi = sb("w_hi", [P, RING, SUB], F32R)
        w_lo = sb("w_lo", [P, RING, SUB], F32R)
        xT_hi = sb("xT_hi", [P, DK, T], F32R)
        xT_lo = sb("xT_lo", [P, DK, T], F32R)
        act_hi = sb("act_hi", [P, DK, T], F32R)
        act_lo = sb("act_lo", [P, DK, T], F32R)
        X = sb("X", [P, TT, D])
        merged = sb("merged", [P, DK, T])
        qT = sb("qT", [P, NH // 2, T])
        kT = sb("kT", [P, 2, NG, T])
        vT = sb("vT", [P, 2, T])
        V = sb("V", [P, 2, TT, P])
        tmp = sb("tmp", [P, 2, T])
        hid = tmp[:, :, :].rearrange("p a t -> p (a t)")
        hidT = sb("hidT", [P, 4, NG * NC])
        hbias = sb("hbias", [P, 4])
        bufA = sb("bufA", [P, 4, T])
        bufB = sb("bufB", [P, 4, T + 2])
        bufC = sb("bufC", [P, 4, T])
        rv = sb("rv", [P, TT, WB])
        rg = sb("rg", [P, 4, T])
        G = sb("G", [P, 4, T])
        soft = sb("soft", [P, 2, D])
        prob, probT = soft[:, 0].rearrange("p (r k) -> p r k", r=NR), soft[:, 1]
        lnp = soft
        cprobT = sb("cprobT", [16, NH * P])
        cprob = sb("cprob", [P, NH, NC])
        ngT = sb("ngT", [3 * NH, T])
        gate = sb("gate", [P, TT, 3 * NH])
        kcT = sb("kcT", [P, NG, NC])
        Vc = sb("Vc", [NC, NG, DH])
        cst = sb("cst", [P, C_W])
        cstf = rg[:, :, :].rearrange("p a t -> p (a t)")[:, 0:B_W]
        cb = sb("cb", [P, B_W], BF16)
        sm = sb("sm", [P, L, S_W])
        stat = sb("stat", [P, 64])
        bst = sb("bst", [P, 8, 6])
        mv = sb("mv", [P, 8, 2])
        rstd = sb("rstd", [P, 8])
        route = sb("route", [P, 640])
        items = sb("items", [P, TT, NI + 1, 2])
        table = sb("table", [1, 16], I32)
        idx8 = sb("idx8", [P, TT, 8], U32)
        chosen_b = sb("chosen_b", [P, TT, NE], BF16)
        eps = sb("eps", [P, 1])
        PS = ctx.enter_context(nc.psum_tensor("PS", [P, 8, 512], F32))

        ident = cst[:, C_ID:C_ID + P]
        decay = cst[:, C_DEC:C_DEC + RH * 256].rearrange("p (h c) -> p h c", h=RH)
        cosT = cst[:, C_COS:C_COS + T]
        sinT = cst[:, C_SIN:C_SIN + T]
        iota = cst[:, C_IOTA:C_IOTA + P]
        iota8 = cst[:, C_IOTA8:C_IOTA8 + NE]
        tri8 = cst[:, C_TRI8:C_TRI8 + NE * NE].rearrange("p (a b) -> p a b", a=NE)
        valid = cst[:, C_VALID:C_VALID + TT * NC].rearrange("p (t n) -> p t n", t=TT)
        identb = cb[:, B_ID:B_ID + P]
        maskb = cb[:, B_MASK:B_MASK + 2 * P]
        cmpb = cb[:, B_CMP:B_CMP + TT * NC].rearrange("p (t n) -> p t n", t=TT)
        before = cb[:, B_LT:B_LT + P]
        ones = cb[:, B_ONE:B_ONE + P]
        z_hi = act_hi[:, :, :].rearrange("p a t -> p (a t)")[:, 0:6 * P]
        z_lo = act_lo[:, :, :].rearrange("p a t -> p (a t)")[:, 0:6 * P]
        zg_hi, zg_lo = (z.rearrange("p (g m) -> p g m", g=6) for z in (z_hi, z_lo))
        rqT, rkT, rvT = bufA, bufB[:, :, 2:T + 2], bufC
        inn = kT[:, :, :, :].rearrange("p a g t -> p (a g t)")[:, 0:768].rearrange("p (b c) -> p b c", b=2)
        onorm = qT[:, :, :].rearrange("p a t -> p (a t)").rearrange("p (t c) -> p t c", t=TT)
        silu, hidden = bufA, bufB[:, :, 2:T + 2]
        silu_e = bufA[:, :, :].rearrange("p a t -> p (a t)")[:, 0:512]
        hidden_e = tmp[:, :, :].rearrange("p a t -> p (a t)")
        y_e = bufC[:, :, :].rearrange("p a t -> p (a t)")
        pick = rv[:, 0, 0:TT * P].rearrange("p (t s) -> p t s", t=TT)
        pickw = rv[:, 0, TT * P:2 * TT * P].rearrange("p (t s) -> p t s", t=TT)
        pickwT = rv[:, 1, 0:T]
        acc = merged[:, :, :].rearrange("p a t -> p (a t)").rearrange("p (t d) -> p t d", t=TT)
        xe_hi = xT_hi[:, :, 0:P]
        xe_lo = xT_lo[:, :, 0:P]
        hT_hi = act_hi[:, :, :].rearrange("p a t -> p (a t)")[:, 0:512]
        hT_lo = act_lo[:, :, :].rearrange("p a t -> p (a t)")[:, 0:512]
        wr_hi = act_hi[:, :, :].rearrange("p a t -> p (a t)")[:, 0:DK * P].rearrange("p (k c) -> p k c", k=DK)
        wr_lo = act_lo[:, :, :].rearrange("p a t -> p (a t)")[:, 0:DK * P].rearrange("p (k c) -> p k c", k=DK)
        wr = bufA[:, :, :].rearrange("p a t -> p (a t)").rearrange("p (k c) -> p k c", k=DK)
        logT = rg[0:NE, 0, :]

        landed = [sem(f"landed{i}") for i in range(RING)]
        hi_done, lo_done = sem("hi_done"), sem("lo_done")
        sub_used = sem("sub_used")
        half_unit = sem("half_unit")
        act_free, dve_free = sem("act_free"), sem("dve_free")
        x_in, const_in, lnp_in, wr_in, out_dma = (sem(n) for n in ("x_in", "const_in", "lnp_in", "wr_in", "out_dma"))
        const_rdy = sem("const_rdy")
        norm_rdy, norm_ps, xT_hi_rdy, xT_rdy = (sem(n) for n in ("norm_rdy", "norm_ps", "xT_hi_rdy", "xT_rdy"))
        z_hi_rdy, vt_ps, v_rdy = sem("z_hi_rdy"), sem("vt_ps"), sem("v_rdy")
        hid_rdy, ht_ps, hbias_rdy, hidT_rdy, w2_ps, kc_rdy = (
            sem(n) for n in ("hid_rdy", "ht_ps", "hbias_rdy", "hidT_rdy", "w2_ps", "kc_rdy"))
        s_ps, max_rdy, exp_rdy, prob_rdy, pt_ps, ptA_rdy, ptD_rdy, av_ps, yA_hi, yA_lo = (
            sem(n) for n in ("s_ps", "max_rdy", "exp_rdy", "prob_rdy", "pt_ps", "ptA_rdy", "ptD_rdy", "av_ps",
                             "yA_hi", "yA_lo"))
        yB_hi, yB_lo = sem("yB_hi"), sem("yB_lo")
        rvt_ps, rv_rdy, rs_ps, inn_rdy, ra_ps, gvar_rdy, gstd_rdy, on_rdy, rt_ps, tanh_rdy, yC_rdy, yC_hi, yC_lo = (
            sem(n) for n in ("rvt_ps", "rv_rdy", "rs_ps", "inn_rdy", "ra_ps", "gvar_rdy", "gstd_rdy", "on_rdy",
                             "rt_ps", "tanh_rdy", "yC_rdy", "yC_hi", "yC_lo"))
        rot_rdy = sem("rot_rdy")
        m_rdy, m_hi, m_lo = sem("m_rdy"), sem("m_hi"), sem("m_lo")
        tok_ps = sem("tok_ps")
        var_rdy, std_rdy = sem("var_rdy"), sem("std_rdy")
        silu_rdy, hid_ff, hT_hi_rdy, hT_rdy = (sem(n) for n in ("silu_rdy", "hid_ff", "hT_hi_rdy", "hT_rdy"))
        wr_hi_rdy, wr_rdy, log_ps, logT_rdy, log2_ps, cnt_in, cnt_ps, table_rdy = (
            sem(n) for n in ("wr_hi_rdy", "wr_rdy", "log_ps", "logT_rdy", "log2_ps", "cnt_in", "cnt_ps", "table_rdy"))
        router_exp, router_exped = sem("router_exp"), sem("router_exped")
        pick_rdy, pickw_rdy, gather_ps, xe_hi_rdy, xe_rdy, wt_ps, wt_rdy = (
            sem(n) for n in ("pick_rdy", "pickw_rdy", "gather_ps", "xe_hi_rdy", "xe_rdy", "wt_ps", "wt_rdy"))
        esilu_rdy, ehid_rdy, et_ps, ehT_hi, ehT_rdy, y_rdy, scat_ps, acc_rdy = (
            sem(n) for n in ("esilu_rdy", "ehid_rdy", "et_ps", "ehT_hi", "ehT_rdy", "y_rdy", "scat_ps", "acc_rdy"))
        act_chain, dve_chain = sem("act_chain"), sem("dve_chain")

        def wait_landed(eng, sub):
            tile = sub // 2
            eng.wait_ge(landed[tile % RING], 16 * (tile // RING + 1))

        def raw_half(slot, half):
            return raw[:, slot, half * SUB:(half + 1) * SUB]

        block = ctx.enter_context(nc.Block())

        @block.sync
        def _(sp):
            sp.dma_start(X[:, :, :], x.rearrange("(t p) d -> p t d", p=P)).then_inc(x_in, 16)
            sp.dma_start(ident, consts[:, C_ID:C_ID + P]).then_inc(x_in, 16)
            for t in range(RING):
                sp.dma_start(raw[:, t], wstream[t]).then_inc(landed[t], 16)
                if t == 0:
                    sp.dma_start(cst[:, P:C_W], consts[:, P:C_W]).then_inc(const_in, 16)
                    sp.dma_start(cstf, constb).then_inc(const_in, 16)
                    sp.dma_start(sm[:, :, :], small.rearrange("l p c -> p l c")).then_inc(const_in, 16)
            rest = NTILES - RING

            def tile(slot, src, index):
                sp.wait_ge(lo_done, 2 * index - 2 * RING + 2)
                sp.dma_start(raw[:, slot], src).then_inc(landed[slot], 16)

            with sp.Fori(0, rest // RING) as i:
                for c in range(RING):
                    t = i * RING + (RING + c)
                    tile(c, wstream[bass.ds(t, 1)].rearrange("a p c -> (a p) c"), t)
            for t in range(RING + rest // RING * RING, NTILES):
                tile(t % RING, wstream[t], t)
            sp.wait_ge(table_rdy, 1)
            extra = sp.value_load(table[0:1, NX:NX + 1], min_val=0, max_val=NX)
            with sp.If(extra > 0):
                with sp.Fori(0, extra) as i:
                    e = sp.value_load(table[0:1, bass.ds(i, 1)], min_val=0, max_val=NE - 1)
                    with sp.Fori(0, ITEM_TILES // RING) as b:
                        for c in range(RING):
                            t = e * ITEM_TILES + b * RING + (MOE0 // 2 + c)
                            tile((NTILES + c) % RING, wstream[bass.ds(t, 1)].rearrange("a p c -> (a p) c"),
                                 i * ITEM_TILES + b * RING + (NTILES + c))
            for c in range(2):
                tile((NTILES + c) % RING, wstream[c], extra * ITEM_TILES + (NTILES + c))

        @block.tensor
        def _(pe):
            mm = nc.tensor.matmul

            def sub_ready(s):
                pe.wait_ge(lo_done, s + 1)

            def fm_unit(bank, slot, chunks, rhs_hi, rhs_lo, nk, cols, middle=None):
                for n, c in enumerate(chunks):
                    if n and middle:
                        middle()
                    o = PS[:, bank, n * T:(n + 1) * T]
                    for k in range(nk):
                        at = slice(k * cols + c * P, k * cols + (c + 1) * P)
                        wh, wl = w_hi[:, slot, at], w_lo[:, slot, at]
                        mm(o, wh, rhs_hi[:, k, :], start=(k == 0), stop=False)
                        mm(o, wh, rhs_lo[:, k, :], start=False, stop=False)
                        last = mm(o, wl, rhs_hi[:, k, :], start=False, stop=(k == nk - 1))
                return last

            def tm_block(outs, slot, lhs, ks, cols, first, final, at=0):
                for bank, tok, c0 in outs:
                    o = PS[:, bank, :]
                    for n, k in enumerate(ks):
                        lh, ll = lhs(k, tok)
                        w0 = (at + n) * cols + c0
                        wh, wl = w_hi[:, slot, w0:w0 + 512], w_lo[:, slot, w0:w0 + 512]
                        mm(o, lh, wh, start=(first and n == 0), stop=False)
                        mm(o, lh, wl, start=False, stop=False)
                        last = mm(o, ll, wh, start=False, stop=(final and n == len(ks) - 1))
                return last

            def last_pair(s, lhs, outs, ks, cols):
                for t in range(TT):
                    for n in range(2):
                        if t == 0:
                            sub_ready(s + n)
                        last = tm_block([o for o in outs if o[1] == t], (s + n) % RING, lhs, ks[n], cols,
                                        cols == 512 and n == 0, n == 1)
                        if t == TT - 1:
                            last.then_inc(sub_used, 1)
                    if t == 0:
                        last.then_inc(tok_ps, 1)

            def to_features(n):
                for t in range(TT):
                    if n == 0:
                        pe.wait_ge(x_in, 32)
                    for k in range(DK):
                        if n and k % 4 == 0:
                            pe.wait_ge(norm_rdy, 2 * TT * (n - 1) + 2 * t + k // 4 + 1)
                        last = nc.tensor.transpose(PS[:, NORM_BANKS[2 * t + k // 4], (k % 4) * P:(k % 4 + 1) * P],
                                                   X[:, t, k * P:(k + 1) * P], ident)
                        if k % 4 == 3:
                            last.then_inc(norm_ps, 1)

            def mixer(l):
                base = LAYER * l

                def unit_free(u):
                    if u >= 2:
                        w = UNITS[u - 2]
                        pe.wait_ge(act_free if w == "act" else dve_free,
                                   unit_count(NU - 1, w) * l + unit_count(u - 2, w))

                def proj(s, u):
                    sub_ready(base + s)
                    unit_free(u)
                    fm_unit(PA[u % 2], (base + s) % RING, (0,) if u == 5 else (0, 1), xT_hi, xT_lo, DK, 2 * P,
                            lambda: attention_between(s)).then_inc(sub_used, 1)

                def compress(s):
                    kv, half = (s - 4) // 2, s % 2
                    sub_ready(base + s)
                    if s == 4:
                        pe.wait_ge(dve_free, unit_count(NU - 1, "dve") * l + 1)
                    slot = (base + s) % RING
                    o = PS[0:ZM, YB, kv * CH:(kv + 1) * CH]
                    for j in range(8):
                        jj = 8 * half + j

                        def z(a):
                            return a[:, kv * P + jj:kv * P + jj + 8 * (ZM - 1) + 1:8]
                        wh, wl = (w[:, slot, j * CH:(j + 1) * CH] for w in (w_hi, w_lo))
                        mm(o, z(z_hi), wh, start=(jj == 0), stop=False)
                        mm(o, z(z_hi), wl, start=False, stop=False)
                        last = mm(o, z(z_lo), wh, start=False, stop=(jj == 15))
                    last.then_inc(sub_used, 1)

                def values_to_tokens():
                    pe.wait_ge(act_free, unit_count(NU - 1, "act") * l + unit_count(5, "act"))
                    pe.wait_ge(dve_free, unit_count(NU - 1, "dve") * l + unit_count(4, "dve"))
                    pe.wait_ge(kc_rdy, l + 1)
                    for a in range(2):
                        for t in range(TT):
                            nc.tensor.transpose(PS[:, MB, (2 * a + t) * P:(2 * a + t + 1) * P],
                                                vT[:, a, t * P:(t + 1) * P], ident)
                    for t in range(TT):
                        last = nc.tensor.transpose(PS[:, TB, t * 24:(t + 1) * 24], ngT[:, t * P:(t + 1) * P],
                                                   ident[0:24, 0:24])
                    last.then_inc(vt_ps, 1)

                def hidden_to_features():
                    pe.wait_ge(hid_rdy, l + 1)
                    for n in range(4):
                        last = nc.tensor.transpose(PS[:, MB, n * ZM:(n + 1) * ZM], hid[0:ZM, n * P:(n + 1) * P],
                                                   ident[0:ZM, 0:ZM])
                    last.then_inc(ht_ps, 1)

                def compressed_kv():
                    pe.wait_ge(const_in, 16 * 3)
                    pe.wait_ge(const_rdy, 2)
                    pe.wait_ge(hidT_rdy, l + 1)
                    for c in range(2):
                        mm(PS[:, MB, 0:NG * NC], sm[:, l, S_W2K + c * P:S_W2K + (c + 1) * P], hidT[:, c, :],
                           start=(c == 0), stop=(c == 1))
                    for g in range(NG):
                        o = PS[0:NC, MB, 64 + g * DH:64 + (g + 1) * DH]
                        for c in range(2):
                            mm(o, hidT[:, 2 + c, g * NC:(g + 1) * NC], sm[:, l, S_W2V + c * DH:S_W2V + (c + 1) * DH],
                               start=(c == 0), stop=False)
                        last = mm(o, one_row, sm[0:1, l, S_B2V:S_B2V + DH], start=False, stop=True)
                    last.then_inc(w2_ps, 1)

                one_row = cst[0:1, C_ONES:C_ONES + NC]

                def query(h, qt):
                    b = (h % 2) * DH
                    return qT[b:b + DH, h // 2, qt * P:(qt + 1) * P]

                def scores(j):
                    kind, qt, g, a = STEPS[j]
                    n = NS * l + j
                    if j:
                        pe.wait_ge(exp_rdy, n)
                    if kind == "cmp":
                        m = cmpb[:, qt, :].unsqueeze(1).broadcast_to([P, NH // 2, NC])
                        for par in range(2):
                            o = PS[:, SB + par, 0:8 * NH].rearrange("p (i n) -> p i n", n=16)[:, :, 0:NC]
                            mm(o, identb, m, start=True, stop=False, skip_group_check=True)
                            for i in range(NH // 2):
                                last = mm(o[:, i, :], query(2 * i + par, qt), kcT[par * DH:(par + 1) * DH, i // 2, :],
                                          start=False, stop=(i == NH // 2 - 1), skip_group_check=True)
                    else:
                        w = (qt + 1) * P
                        m = maskb[:, 2 * P - w:2 * P].unsqueeze(1).broadcast_to([P, 2, w])
                        for par in range(2):
                            o = PS[:, SB + par, :].rearrange("p (i k) -> p i k", i=2)
                            mm(o[:, :, 0:w], identb, m, start=True, stop=False, skip_group_check=True)
                            for i in range(2):
                                last = mm(o[:, i, 0:w], query(NR * g + 2 * i + par, qt),
                                          kT[par * DH:(par + 1) * DH, a, g, 0:w], start=False, stop=(i == 1),
                                          skip_group_check=True)
                    last.then_inc(s_ps, 1)

                def transposes(j):
                    kind, qt, g, a = STEPS[j]
                    pe.wait_ge(prob_rdy, NS * l + j + 1)
                    if kind == "cmp":
                        for n in range(NH):
                            last = mm(PS[0:NC, TB + n // 4, (n % 4) * P:(n % 4 + 1) * P], cprob[:, n, :], ident,
                                      start=True, stop=True)
                    else:
                        for kb in range(qt + 1):
                            for r in range(NR):
                                last = nc.tensor.transpose(PS[:, TB + kb, r * P:(r + 1) * P],
                                                           prob[:, r, kb * P:(kb + 1) * P], ident)
                    last.then_inc(pt_ps, 1)

                def weighted(j):
                    kind, qt, g, a = STEPS[j]
                    n = NS * l + j + 1
                    pe.wait_ge(ptA_rdy, n)
                    pe.wait_ge(ptD_rdy, second_banks(NS - 1) * l + second_banks(j))
                    if kind == "cmp":
                        return
                    if a == 0:
                        pe.wait_ge(yA_lo, len(GROUP_ENDS) * l + sum(e < j for e in GROUP_ENDS))
                    for par in range(2):
                        o = PS[par * DH:(par + 1) * DH, YB, 0:2 * P]
                        for kb in range(qt + 1):
                            last = mm(o, V[:, a, kb, g * DH:(g + 1) * DH], probT[:, kb * 512 + par * 256:kb * 512 + (par + 1) * 256],
                                      start=(a == 0 and kb == 0), stop=False, skip_group_check=True)
                        if a == 1:
                            last = mm(o, Vc[:, g, :], cprobT[0:NC, (4 * par + 2 * g) * P:(4 * par + 2 * g + 2) * P], start=False,
                                      stop=True, skip_group_check=True)
                    last.then_inc(av_ps, 1)

                def ret_values(t):
                    if t == 0:
                        pe.wait_ge(act_free, unit_count(NU - 1, "act") * l + unit_count(U_RV + 1, "act"))
                    else:
                        pe.wait_ge(rv_rdy, TT * l + t)
                    for h in range(RH):
                        last = nc.tensor.transpose(PS[:, MB, h * P:(h + 1) * P], rvT[:, h, t * P:(t + 1) * P], ident)
                    last.then_inc(rvt_ps, 1)

                def ret_scores(h):
                    bank = SB + h % 2
                    if h >= 2:
                        pe.wait_ge(inn_rdy, RH * l + h - 1)
                    elif h == 0:
                        pe.wait_ge(rot_rdy, 4 * (l + 1))
                    mm(PS[:, bank, 0:T], rkT[:, h, 0:P], rqT[:, h, :], start=True, stop=True)
                    mm(PS[:, bank, T:T + P], rkT[:, h, P:T], rqT[:, h, P:T], start=True, stop=True).then_inc(rs_ps, 1)

                def ret_sums(h):
                    pe.wait_ge(inn_rdy, RH * l + h + 1)
                    if h == 0:
                        pe.wait_ge(rv_rdy, TT * l + TT)
                    b, cols = h % 2, slice(h * P, (h + 1) * P)
                    mm(PS[:, TB, cols], inn[:, b, 0:P], rv[:, 0, cols], start=True, stop=True)
                    mm(PS[:, TB + 1, cols], inn[:, b, P:2 * P], rv[:, 0, cols], start=True, stop=False)
                    mm(PS[:, TB + 1, cols], inn[:, b, 2 * P:3 * P], rv[:, 1, cols], start=False,
                       stop=True).then_inc(ra_ps, 1)

                def ret_to_features():
                    pe.wait_ge(on_rdy, l + 1)
                    for h in range(RH):
                        for t in range(TT):
                            last = nc.tensor.transpose(
                                PS[:, SB + h // 2, (h % 2) * T + t * P:(h % 2) * T + (t + 1) * P],
                                onorm[:, t, h * P:(h + 1) * P], ident)
                    last.then_inc(rt_ps, 1)

                def branch(s, b):
                    half = (s - BRANCH0 - 6 * b) // 5
                    u = U_BR + 8 * b + 2 + 4 * half
                    sub_ready(base + s)
                    if half == 0:
                        pe.wait_ge(*[(yB_lo, l + 1), (yA_lo, len(GROUP_ENDS) * (l + 1)), (yC_lo, l + 1)][b])
                    slots = slice(4 if b == MID_BRANCH else 0, 8 if b == MID_BRANCH else 4)
                    for n in range(2):
                        if n:
                            attention_between(s)
                        unit_free(u + n)
                        last = fm_unit(PA[(u + n) % 2], (base + s) % RING, (2 * n, 2 * n + 1), act_hi[:, slots],
                                       act_lo[:, slots], 4, 512)
                        last.then_inc(half_unit if n == 0 else sub_used, 1)

                def project_out(s):
                    def lhs(k, t):
                        c = (k + 4) % DK
                        return act_hi[:, c, t * P:(t + 1) * P], act_lo[:, c, t * P:(t + 1) * P]
                    if s < OUT0 + 2:
                        kh = s % 2
                        sub_ready(base + s)
                        pe.wait_ge(m_lo, 4 * l + 2 * kh + 2)
                        tm_block([(SB, 0, 0), (TB, 1, 0)], (base + s) % RING, lhs,
                                 range(4 * kh, 4 * kh + 4), 512, kh == 0, kh == 1).then_inc(sub_used, 1)
                    elif s == OUT0 + 2:
                        last_pair(base + s, lhs, [(SB + 1, 0, 0), (TB + 1, 1, 0)], (range(4), range(4, 8)), 512)

                def attention_between(s):
                    j, late = divmod(s - STEP0, 2)
                    if 0 <= s - STEP0 <= 2 * NS:
                        if late:
                            transposes(j)
                        elif j:
                            weighted(j - 1)

                pe.wait_ge(xT_rdy, TT * 2 * (2 * l + 1))
                for s in range(MIX):
                    if s == 9:
                        hidden_to_features()
                    if s == 10:
                        compressed_kv()
                    if s == 11:
                        values_to_tokens()
                    if STEP0 <= s < STEP0 + 2 * NS and (s - STEP0) % 2 == 0:
                        scores((s - STEP0) // 2)
                    if s in (23, 25):
                        ret_values((s - 23) // 2)
                    if s == RET0:
                        ret_scores(0)
                        ret_scores(1)
                    if s == RET0 + 1:
                        ret_sums(0)
                        ret_sums(1)
                        ret_scores(2)
                        ret_scores(3)
                    if s == RET0 + 2:
                        ret_sums(2)
                        ret_sums(3)
                    if s == RET0 + 4:
                        ret_to_features()
                    if s < 4:
                        proj(s, s)
                    elif s < 8:
                        compress(s)
                    elif s < BRANCH0:
                        proj(s, s - 4)
                    elif s < OUT0:
                        b, n = divmod(s - BRANCH0, 6)
                        if n in (2, 5):
                            branch(s, b)
                        else:
                            proj(s, U_BR + 8 * b + (n if n < 2 else n + 1))
                    else:
                        project_out(s)

            def dense():
                f0 = MIX

                def up(b, s, which, first=False):
                    banks = (0, 1) if which == "gate" else (6, 7)
                    for n in range(2):
                        sub_ready(s + n)
                        if not first:
                            pe.wait_ge(silu_rdy if which == "gate" else hid_ff, b * 2 + (n - 1))
                        fm_unit(banks[n], (static[0] + n) % RING, (0, 1), xT_hi, xT_lo, DK,
                                2 * P).then_inc(sub_used, 1)
                    static[0] += 2

                def down(b, s, first=False, final=False):
                    def lhs(k, t):
                        return act_hi[:, k, t * P:(t + 1) * P], act_lo[:, k, t * P:(t + 1) * P]
                    outs = [(SB + 2 * t + c, t, 512 * c) for t in range(TT) for c in range(2)]
                    if final:
                        pe.wait_ge(hT_rdy, 2 * b + 2)
                        last_pair(s, lhs, outs, ((0, 1), (2, 3)), 1024)
                        return
                    for n in range(2):
                        sub_ready(s + n)
                        pe.wait_ge(hT_rdy, 2 * b + n + 1)
                        tm_block(outs, (static[0] + n) % RING, lhs, (2 * n, 2 * n + 1), 1024, first and n == 0,
                                 False).then_inc(sub_used, 1)
                    static[0] += 2

                static = [f0]
                pe.wait_ge(xT_rdy, TT * 2 * 2)
                up(0, f0, "gate", True)
                up(0, f0 + 2, "up", True)
                up(1, f0 + 4, "gate")
                down(0, f0 + 6, first=True)
                with pe.Fori(1, NB - 1) as b:
                    s = b * 6 + (f0 + 2)
                    up(b, s, "up")
                    up(b + 1, s + 2, "gate")
                    down(b, s + 4)
                b = NB - 1
                up(b, f0 + 2 + 6 * b, "up")
                down(b, f0 + 4 + 6 * b, final=True)

            def router_logits():
                pe.wait_ge(xT_rdy, TT * 2 * 4)
                pe.wait_ge(wr_rdy, 1)
                for k in range(DK):
                    mm(PS[:, 0, 0:T], wr_hi[:, k, :], xT_hi[:, k, :], start=(k == 0), stop=False)
                    mm(PS[:, 0, 0:T], wr_hi[:, k, :], xT_lo[:, k, :], start=False, stop=False)
                    last = mm(PS[:, 0, 0:T], wr_lo[:, k, :], xT_hi[:, k, :], start=False, stop=(k == DK - 1))
                last.then_inc(log_ps, 1)
                pe.wait_ge(logT_rdy, 1)
                for t in range(TT):
                    last = nc.tensor.transpose(PS[:, 1, t * NE:(t + 1) * NE], logT[:, t * P:(t + 1) * P],
                                               ident[0:NE, 0:NE])
                last.then_inc(log2_ps, 1)
                pe.wait_ge(cnt_in, 1)
                m = [chosen_b[:, t, :] for t in range(TT)]
                mm(PS[:, 0, 0:NE], before, m[0], start=True, stop=True)
                mm(PS[:, 0, NE:2 * NE], before, m[1], start=True, stop=False)
                mm(PS[:, 0, NE:2 * NE], ones, m[0], start=False, stop=True)
                mm(PS[:, 0, 2 * NE:3 * NE], ones, m[0], start=True, stop=False)
                mm(PS[:, 0, 2 * NE:3 * NE], ones, m[1], start=False, stop=True).then_inc(cnt_ps, 1)

            def gather(i, ks=range(DK)):
                if ks[0] == 0:
                    pe.wait_ge(pick_rdy, i + 1)
                for k in ks:
                    for t in range(TT):
                        last = mm(PS[:, TB + k // 4, (k % 4) * P:(k % 4 + 1) * P], X[:, t, k * P:(k + 1) * P],
                                  pick[:, t, :], start=(t == 0), stop=(t == TT - 1))
                    if k % 4 == 3:
                        last.then_inc(gather_ps, 1)

            def experts():
                gather(0)
                pe.wait_ge(table_rdy, 1)
                n_items = pe.value_load(table[0:1, NX + 1:NX + 2], min_val=NE, max_val=NI)

                def lhs_x(k, t):
                    return xe_hi[:, k, :], xe_lo[:, k, :]

                def lhs_h(k, t):
                    return hT_hi[:, k * P:(k + 1) * P], hT_lo[:, k * P:(k + 1) * P]

                def up_half(s, at, bank, n, middle=None):
                    sub_ready(s)
                    for m, ks in enumerate((range(4 * n, 4 * n + 3), range(4 * n + 3, 4 * n + 4))):
                        last = tm_block([(bank, 0, 0)], at % RING, lhs_x, ks, 512, n == 0 and m == 0,
                                        n == 1 and m == 1, at=3 * m)
                        if m == 0 and middle:
                            middle()
                    last.then_inc(sub_used, 1)

                def hidden_transposes(n):
                    pe.wait_ge(ehid_rdy, n + 1)
                    for c in range(4):
                        last = nc.tensor.transpose(PS[:, YB, c * P:(c + 1) * P], hidden_e[:, c * P:(c + 1) * P], ident)
                    last.then_inc(et_ps, 1)

                def up(s, at):
                    for h in range(2):
                        up_half(s + h, at + h, 1, h)

                def down(n, s, at, first, final):
                    pe.wait_ge(ehT_rdy, n + 1)
                    for h in range(2):
                        sub_ready(s + h)
                        tm_block([(SB + c, 0, 512 * c) for c in range(2)], (at + h) % RING, lhs_h,
                                 (2 * h, 2 * h + 1), 1024, first and h == 0, final and h == 1).then_inc(sub_used, 1)

                def weights_to_slots(i):
                    pe.wait_ge(pickw_rdy, i + 1)
                    pe.wait_ge(acc_rdy, i * 4 + 2)
                    for t in range(TT):
                        last = nc.tensor.transpose(PS[:, MB, t * P:(t + 1) * P], pickw[:, t, :], ident)
                    last.then_inc(wt_ps, 1)

                def body(n, s, at, item=None):
                    first = item is not None
                    up(s, at)
                    if first:
                        weights_to_slots(item)
                    pe.wait_ge(esilu_rdy, n + 1)
                    up_half(s + 2, at + 2, 0, 0, lambda: hidden_transposes(n))
                    up_half(s + 3, at + 3, 0, 1)
                    down(n, s + 4, at + 4, first, False)

                def scatter(i):
                    pe.wait_ge(wt_rdy, i + 1)
                    pe.wait_ge(y_rdy, i + 1)
                    for n in range(4):
                        t, c = divmod(n, 2)
                        mm(PS[:, SCATTER[n], :], pickwT[:, t * P:(t + 1) * P],
                           y_e[:, c * 512:(c + 1) * 512], start=True, stop=True).then_inc(scat_ps, 1)

                with pe.Fori(0, n_items) as i:
                    s0 = i * FFN + MOE0
                    pe.wait_ge(xe_rdy, i * 2 + 2)
                    up_half(s0, MOE0, 0, 0)
                    up_half(s0 + 1, MOE0 + 1, 0, 1)
                    scatter(i)
                    body(i * NB, s0 + 2, MOE0 + 2, i)
                    with pe.Fori(1, NB - 1) as b:
                        body(i * NB + b, s0 + b * 6 + 2, MOE0 + 2)
                    n = i * NB + (NB - 1)
                    up(s0 + (FFN - 4), MOE0 + 2)
                    gather(i + 1, range(DK // 2))
                    hidden_transposes(n)
                    gather(i + 1, range(DK // 2, DK))
                    down(n, s0 + (FFN - 2), MOE0 + 4, False, True)
                pe.wait_ge(xe_rdy, n_items * 2 + 2)
                scatter(n_items)

            to_features(0)
            mixer(0)
            to_features(1)
            dense()
            to_features(2)
            mixer(1)
            to_features(3)
            router_logits()
            experts()

        @block.scalar
        def _(act):
            activate = nc.scalar.activation
            chain = Chain(act, act_chain)

            def split(at, k=0):
                if at % 2 == 0:
                    act.wait_ge(landed[at // 2 % RING], (k + (at // 6 + 1)) * 16)
                if at >= RING:
                    act.wait_ge(sub_used, k * 6 + (at - RING + 1))
                activate(w_hi[:, at % RING], raw_half(at // 2 % RING, at % 2), ACT.Copy).then_inc(hi_done, 1)

            def norm(n):
                for t in range(TT if n else 0):
                    act.wait_ge(var_rdy, TT * (n - 1) + t + 1)
                    activate(rstd[:, t:t + 1], mv[:, t, 1:2], ACT.Sqrt, bias=eps[:, :]).then_inc(std_rdy, 1)
                    if n < 4:
                        split(NEXT[n] - 2 + t + RING)
                if n == 3:
                    act.wait_ge(wr_in, 16)
                    activate(wr_hi, wr, ACT.Copy).then_inc(wr_hi_rdy, 1)
                if n < 4:
                    for b in range(4):
                        act.wait_ge(norm_ps, 4 * n + b + 1)
                        t, c = divmod(b, 2)
                        activate(xT_hi[:, 4 * c:4 * c + 4, t * P:(t + 1) * P],
                                 PS[:, NORM_BANKS[b], :].rearrange("p (k t) -> p k t", k=4),
                                 ACT.Copy).then_inc(xT_hi_rdy, 1)

            def load_norm(n):
                act.dma_start(lnp[:, :, :], ln[n - 1].partition_broadcast(P)).then_inc(lnp_in, 16)

            def mixer(l):
                base = LAYER * l

                def pa(u):
                    return PS[:, PA[u % 2], :].rearrange("p (c t) -> p c t", c=2)

                def after(s):
                    sub = OUT0 > s >= BRANCH0
                    if not (s in (0, 1, 2, 3, 7, 9, 10, 11, 15, 20, 21, 22, 23) or sub):
                        return
                    act.wait_ge(hi_done, base + s + RING)
                    act.wait_ge(sub_used, base + s + 1)
                    if s < 2:
                        activate(qT[:, 2 * s:2 * s + 2], pa(s), ACT.Copy).then_inc(act_free, 1)
                    elif s == 2:
                        for kv in range(2):
                            activate(zg_hi[:, 3 * kv + 2, :], sm[:, l, S_POS + kv * P:S_POS + (kv + 1) * P], ACT.Copy)
                        for g in range(NG):
                            for par in range(2):
                                last = activate(zg_hi[par * DH:(par + 1) * DH, g::3, :],
                                                pa(2)[g * DH:(g + 1) * DH, :, par::2], ACT.Copy)
                        last.then_inc(z_hi_rdy, 1)
                    elif s == 3:
                        for g in range(NG):
                            for half in range(2):
                                activate(kT[half * DH:(half + 1) * DH, 0, g, :], pa(3)[g * DH:(g + 1) * DH, 0, :],
                                         ACT.Copy)
                        activate(vT[:, 0, :], pa(3)[:, 1, :], ACT.Copy).then_inc(act_free, 1)
                    elif s == 9:
                        activate(ngT[:, :], pa(5)[0:3 * NH, 0, :], ACT.Tanh, scale=0.5).then_inc(act_free, 1)
                    elif s == 7:
                        activate(hid[0:ZM, :], PS[0:ZM, YB, :], ACT.Copy).then_inc(hid_rdy, 1)
                    elif s in (10, 11):
                        c = 2 * (s - 10)
                        activate(bufA[:, c:c + 2], pa(s), ACT.Copy).then_inc(act_free, 1)
                    elif s == 15:
                        act.wait_ge(dve_free, unit_count(NU - 1, "dve") * l + unit_count(U_CONV_B + 1, "dve"))
                        activate(act_hi[:, 0:4], bufC[:, :, :], ACT.Copy).then_inc(yB_hi, 1)
                    elif s in (20, 21):
                        c = 2 * (s - 20)
                        act.wait_ge(yB_lo, l + 1)
                        activate(rvT[:, c:c + 2], pa(s), ACT.Copy).then_inc(act_free, 1)
                    elif s in (22, 23):
                        c = 2 * (s - 22)
                        activate(rg[:, c:c + 2], pa(s), ACT.Copy).then_inc(act_free, 1)
                    else:
                        b, n = divmod(s - BRANCH0, 6)
                        if n in (2, 5):
                            if b == LAST_BRANCH:
                                merged_hi(n // 5)
                            return
                        u = U_BR + 8 * b + (n if n < 2 else n + 1)
                        c = 2 * (n % 3)
                        if s > BRANCH0 + 1:
                            last = U_BR + 8 * b + (-2 if n < 2 else 2) + c // 2
                            act.wait_ge(dve_free, unit_count(NU - 1, "dve") * l + unit_count(last, "dve"))
                        activate(G[:, c:c + 2], pa(u), ACT.Tanh, scale=0.5).then_inc(act_free, 1)

                def merged_hi(half):
                    for n in range(2):
                        act.wait_ge(m_rdy, 4 * l + 2 * half + n + 1)
                        c = 4 * half + 2 * n
                        s = (c + 4) % DK
                        activate(act_hi[:, s:s + 2], merged[:, c:c + 2], ACT.Copy, scale=0.5).then_inc(m_hi, 1)

                def exps(j):
                    kind, qt, g, a = STEPS[j]
                    act.wait_ge(max_rdy, NS * l + j + 1)
                    if kind == "cmp":
                        activate(cprob[:, :, :], cprob[:, :, :], ACT.Exp, scale=DH ** -0.5).then_inc(exp_rdy, 1)
                        return
                    if j:
                        act.wait_ge(pt_ps, NS * l + j)
                    w = (qt + 1) * P
                    for r in range(NR):
                        last = activate(prob[:, r, 0:w], PS[:, SB + r // 2, (r % 2) * T:(r % 2) * T + w], ACT.Exp,
                                        bias=stat[:, 8 + r:9 + r], scale=DH ** -0.5, accum_out=stat[:, 16 + r:17 + r])
                    last.then_inc(exp_rdy, 1)

                def drain_transposes(j):
                    kind, qt, g, a = STEPS[j]
                    act.wait_ge(pt_ps, NS * l + j + 1)
                    if kind == "cmp":
                        activate(cprobT[0:NC, 0:512], PS[0:NC, TB, :], ACT.Copy).then_inc(ptA_rdy, 1)
                    else:
                        activate(probT[:, 0:512], PS[:, TB, :], ACT.Copy).then_inc(ptA_rdy, 1)

                def drain_group(j):
                    kind, qt, g, a = STEPS[j]
                    act.wait_ge(av_ps, 8 * l + sum(s[0] == "full" for s in STEPS[:j + 1]))
                    activate(act_hi[:, 4 + 2 * g:6 + 2 * g, qt * P:(qt + 1) * P],
                             PS[:, YB, 0:2 * P].rearrange("p (c t) -> p c t", c=2), ACT.Copy).then_inc(yA_hi, 1)

                def after_hidden():
                    act.wait_ge(hbias_rdy, l + 1)
                    for n in range(4):
                        off = ZM * n + 32 * (n // 2)
                        last = activate(hidT[:, n, :].rearrange("p (g c) -> p g c", g=NG),
                                        PS[:, MB, off:off + 32].rearrange("p (g c) -> p g c", g=NG)[:, :, 0:NC], ACT.Gelu_apprx_tanh,
                                        bias=hbias[:, n:n + 1])
                    last.then_inc(hidT_rdy, 1)

                for s in range(MIX):
                    after(s)
                    if s < MIX - 2:
                        split(base + s + RING)
                    if l == 1 and s == OUT0:
                        act.dma_start(wr, router).then_inc(wr_in, 16)
                    if s == 8:
                        after_hidden()
                    if s == 10:
                        act.wait_ge(vt_ps, l + 1)
                        activate(V[:, :, :, :].rearrange("p a t c -> p (a t c)"), PS[:, MB, :], ACT.Copy)
                        activate(gate[:, :, :].rearrange("p t c -> p (t c)"), PS[:, TB, 0:TT * 24], ACT.Copy,
                                 bias=0.5, scale=0.5).then_inc(v_rdy, 1)
                    if STEP0 - 1 <= s <= STEP0 + 2 * NS:
                        j, late = divmod(s + 1 - STEP0, 2)
                        if late:
                            if j - 1 in GROUP_ENDS:
                                drain_group(j - 1)
                            if j < NS:
                                drain_transposes(j)
                        elif j < NS:
                            exps(j)
                    if s in (22, 24):
                        t = (s - 22) // 2
                        act.wait_ge(rvt_ps, TT * l + t + 1)
                        activate(rv[:, t, :], PS[:, MB, :], ACT.Copy).then_inc(rv_rdy, 1)
                    if s == RET0:
                        load_norm(2 * l + 1)
                    if s == RET0 + 1:
                        act.wait_ge(rs_ps, RH * (l + 1))
                        activate(rkT, rg[:, :, :], ACT.Tanh, scale=0.5).then_inc(tanh_rdy, 1)
                        act.wait_ge(gvar_rdy, l + 1)
                        activate(rstd[:, 0:8], mv[:, 0:8, 1], ACT.Sqrt, bias=eps[:, :]).then_inc(gstd_rdy, 1)
                    if s == RET0 + 3:
                        act.wait_ge(yC_rdy, l + 1)
                        activate(act_hi[:, 0:4], bufC[:, :, :], ACT.Copy).then_inc(yC_hi, 1)

            def dense():
                f0 = MIX

                def silu_half(b, s, n, first=False):
                    act.wait_ge(sub_used, s + 1)
                    if not first:
                        act.wait_ge(hid_ff, b * 2 + (n - 1))
                    activate(silu[:, 2 * n:2 * n + 2], PS[:, n, :].rearrange("p (c t) -> p c t", c=2),
                             ACT.Silu).then_inc(silu_rdy, 1)

                def hidden_half(b, n):
                    act.wait_ge(hid_ff, b * 2 + (n + 1))
                    activate(act_hi[:, 2 * n:2 * n + 2], hidden[:, 2 * n:2 * n + 2], ACT.Copy).then_inc(hT_hi_rdy, 1)

                def body(b, k, at):
                    for c in range(6):
                        if c < 2:
                            hidden_half(b, c)
                        elif c < 4:
                            silu_half(b + 1, k * 6 + (at + c), c - 2)
                        split(at + c + RING, k)

                for n in range(2):
                    silu_half(0, f0 + n, n, True)
                    split(f0 + n + RING)
                body(0, 0, f0 + 2)
                with act.Fori(1, NB - 1) as b:
                    body(b, b - 1, f0 + 8)
                for c in range(2):
                    hidden_half(NB - 1, c)
                    split(f0 + FFN - 4 + c + RING)

            def experts():
                def gather(i):
                    for c in range(2):
                        act.wait_ge(gather_ps, i * 2 + (c + 1))
                        activate(xe_hi[:, 4 * c:4 * c + 4, :], PS[:, TB + c, :].rearrange("p (k t) -> p k t", k=4),
                                 ACT.Copy).then_inc(xe_hi_rdy, 1)

                def silu_block(n, s):
                    act.wait_ge(sub_used, s + 1)
                    activate(silu_e, PS[:, 0, :], ACT.Silu).then_inc(esilu_rdy, 1)

                def hidden_block(n):
                    act.wait_ge(et_ps, n + 1)
                    activate(hT_hi, PS[:, YB, :], ACT.Copy).then_inc(ehT_hi, 1)

                def body(n, k, s, item=None):
                    for c in range(6):
                        if c == 2:
                            if item is not None:
                                act.wait_ge(wt_ps, item + 1)
                                activate(pickwT, PS[:, MB, 0:T], ACT.Copy).then_inc(wt_rdy, 1)
                            hidden_block(n)
                        split(MOE0 + 2 + c + RING, k)
                        if c == 3:
                            silu_block(n + 1, s + c)

                activate(y_e, cst[:, 0:D], ACT.Copy, scale=0.0).then_inc(y_rdy, 1)
                gather(0)
                act.wait_ge(table_rdy, 1)
                n_items = act.value_load(table[0:1, NX + 1:NX + 2], min_val=NE, max_val=NI)
                activate(pickwT, cst[:, 0:T], ACT.Copy, scale=0.0).then_inc(wt_rdy, 1)
                with act.Fori(0, n_items) as i:
                    s0 = i * FFN + MOE0
                    split(MOE0 + RING, i * NB)
                    split(MOE0 + 1 + RING, i * NB)
                    silu_block(i * NB, s0 + 1)
                    body(i * NB, i * NB, s0 + 2, i)
                    with act.Fori(1, NB - 1) as b:
                        body(i * NB + b, i * NB + b, s0 + b * 6 + 2)
                    k = i * NB + (NB - 1)
                    split(MOE0 + 2 + RING, k)
                    split(MOE0 + 3 + RING, k)
                    hidden_block(k)
                    gather(i + 1)
                    split(MOE0 + 4 + RING, k)
                    split(MOE0 + 5 + RING, k)
                    act.wait_ge(sub_used, s0 + FFN)
                    activate(y_e, PS[:, SB:SB + 2, :].rearrange("p a c -> p (a c)"), ACT.Copy).then_inc(y_rdy, 1)

            act.wait_ge(const_rdy, 1)
            norm(0)
            for s in range(RING):
                split(s)
            act.wait_ge(const_in, 16 * 3)
            mixer(0)
            norm(1)
            act.wait_ge(norm_rdy, 2 * TT)
            load_norm(2)
            dense()
            norm(2)
            mixer(1)
            norm(3)
            act.wait_ge(norm_rdy, 2 * TT * 3)
            load_norm(4)
            act.wait_ge(log_ps, 1)
            activate(logT, PS[0:NE, 0, 0:T], ACT.Copy).then_inc(logT_rdy, 1)
            act.wait_ge(router_exp, 1)
            activate(route[:, 96:98], route[:, 98:100], ACT.Exp).then_inc(router_exped, 1)
            experts()
            norm(4)
            for t in range(TT):
                act.wait_ge(norm_rdy, 2 * TT * 3 + 2 * t + 2)
                act.dma_start(out[t * P:(t + 1) * P, :], X[:, t, :]).then_inc(out_dma, 16)
            act.wait_ge(out_dma, 16 * TT)

        @block.vector
        def _(dve):
            v = nc.vector
            chain = Chain(dve, dve_chain)

            def split(at, k=0):
                dve.wait_ge(hi_done, k * 6 + (at + 1))
                v.tensor_tensor(w_lo[:, at % RING], raw_half(at // 2 % RING, at % 2), w_hi[:, at % RING],
                                ALU.subtract).then_inc(lo_done, 1)

            def add_x(n, t, c):
                o = X[:, t, c * 512:(c + 1) * 512]
                return v.scalar_tensor_tensor(o, o, ALPHA, PS[:, SB + 2 * t + c, :], ALU.mult, ALU.add)

            def stats(n, t, c):
                src = X if n < 4 else acc
                return v.bn_stats(bst[:, 2 * t + c, :], src[:, t, c * 512:(c + 1) * 512])

            def norm_tokens(n, t):
                halves = (0, 1) if n % 2 == 0 else (1,)
                if n < 4:
                    if t == 0:
                        dve.wait_ge(tok_ps, n)
                    else:
                        dve.wait_ge(sub_used, NEXT[n])
                    for c in halves:
                        last = add_x(n, t, c)
                    chain.link(last)
                src = X if n < 4 else acc
                for c in halves:
                    last = stats(n, t, c)
                chain.link(last)
                v.bn_aggr(mv[:, t, :], bst[:, 2 * t:2 * t + 2, :].rearrange("p a b -> p (a b)")).then_inc(var_rdy, 1)
                dve.wait_ge(std_rdy, TT * (n - 1) + t + 1)
                chain.link(v.reciprocal(rstd[:, t:t + 1], rstd[:, t:t + 1]))
                dve.wait_ge(lnp_in, 16 * n)
                cs = [slice(c * 512, (c + 1) * 512) for c in range(2)]
                for c in cs:
                    last = v.scalar_tensor_tensor(X[:, t, c], src[:, t, c], mv[:, t, 0:1], lnp[:, 0, c],
                                                  ALU.subtract, ALU.mult)
                chain.link(last)
                for c in cs:
                    v.scalar_tensor_tensor(X[:, t, c], X[:, t, c], rstd[:, t:t + 1], lnp[:, 1, c], ALU.mult,
                                           ALU.add).then_inc(norm_rdy, 1)

            def norm(n):
                for t in range(TT if n else 0):
                    norm_tokens(n, t)
                if n == 3:
                    dve.wait_ge(wr_hi_rdy, 1)
                    v.tensor_tensor(wr_lo, wr, wr_hi, ALU.subtract).then_inc(wr_rdy, 1)
                if n < 4:
                    for b in range(4):
                        t, c = divmod(b, 2)
                        dve.wait_ge(xT_hi_rdy, 4 * n + b + 1)
                        at = (slice(None), slice(4 * c, 4 * c + 4), slice(t * P, (t + 1) * P))
                        v.tensor_tensor(xT_lo[at], PS[:, NORM_BANKS[b], :].rearrange("p (k t) -> p k t", k=4),
                                        xT_hi[at], ALU.subtract).then_inc(xT_rdy, 1)
                    if n:
                        for t in range(2):
                            split(NEXT[n] - 2 + t + RING)

            def mixer(l):
                base = LAYER * l

                def pa(u):
                    return PS[:, PA[u % 2], :].rearrange("p (c t) -> p c t", c=2)

                def conv(k):
                    for c in range(4):
                        w = sm[:, l, S_CONV + 4 * k + c:S_CONV + 4 * k + c + 1]
                        if k == 2:
                            last = v.tensor_scalar(bufC[:, c, :], bufB[:, c, 2:T + 2], w, None, ALU.mult)
                        else:
                            last = v.scalar_tensor_tensor(bufC[:, c, :], bufB[:, c, k:T + k], w, bufC[:, c, :],
                                                          ALU.mult, ALU.add)
                    chain.link(last)

                def rotary(dst, u):
                    cos = cosT.unsqueeze(1).broadcast_to([P, 2, T])
                    sin = sinT.unsqueeze(1).broadcast_to([P, 2, T])
                    v.tensor_tensor(dst, pa(u), cos, ALU.mult)
                    v.tensor_tensor(tmp[0:64], pa(u)[64:128], sin[64:128], ALU.mult)
                    v.tensor_tensor(tmp[64:128], pa(u)[0:64], sin[0:64], ALU.mult).then_inc(dve_free, 1)
                    dve.wait_ge(dve_free, unit_count(NU - 1, "dve") * l + unit_count(u, "dve"))
                    v.tensor_tensor(dst, dst, tmp[:, :, :], ALU.add).then_inc(rot_rdy, 1)

                def gated(u, b, c):
                    g = G[:, c % 4:c % 4 + 2]
                    if b == FIRST_BRANCH:
                        v.scalar_tensor_tensor(merged[:, c:c + 2], g, 1.0, pa(u), ALU.add,
                                               ALU.mult).then_inc(dve_free, 1)
                        return
                    v.scalar_tensor_tensor(tmp[:, :, :], g, 1.0, pa(u), ALU.add, ALU.mult).then_inc(dve_free, 1)
                    dve.wait_ge(dve_free, unit_count(NU - 1, "dve") * l + unit_count(u, "dve"))
                    o = merged[:, c:c + 2]
                    if b == LAST_BRANCH:
                        v.tensor_tensor(o, o, tmp[:, :, :], ALU.add).then_inc(m_rdy, 1)
                        dve.wait_ge(m_rdy, 4 * l + c // 2 + 1)
                    else:
                        chain.link(v.tensor_tensor(o, o, tmp[:, :, :], ALU.add))

                def after(s):
                    if s >= OUT0:
                        if s == OUT0 + 1:
                            dve.wait_ge(sub_used, base + s + 1)
                            for t in range(TT):
                                last = add_x(2 * l + 1, t, 0)
                            chain.link(last)
                            for t in range(TT):
                                last = stats(2 * l + 1, t, 0)
                            chain.link(last)
                        return
                    dve.wait_ge(lo_done, base + s + RING)
                    if s in (2, 8, 12, 13, 14, 15, 16, 17, 18, 19):
                        dve.wait_ge(sub_used, base + s + 1)
                    if s == 2:
                        dve.wait_ge(z_hi_rdy, l + 1)
                        for kv in range(2):
                            v.tensor_tensor(zg_lo[:, 3 * kv + 2, :], sm[:, l, S_POS + kv * P:S_POS + (kv + 1) * P],
                                            zg_hi[:, 3 * kv + 2, :], ALU.subtract)
                        for g in range(NG):
                            for par in range(2):
                                q = slice(par * DH, (par + 1) * DH)
                                last = v.tensor_tensor(zg_lo[q, g::3, :], pa(2)[g * DH:(g + 1) * DH, :, par::2],
                                                       zg_hi[q, g::3, :], ALU.subtract)
                        last.then_inc(dve_free, 1)
                    elif s == 8:
                        for g in range(NG):
                            for half in range(2):
                                v.tensor_copy(kT[half * DH:(half + 1) * DH, 1, g, :], pa(4)[g * DH:(g + 1) * DH, 0, :])
                        v.tensor_copy(vT[:, 1, :], pa(4)[:, 1, :]).then_inc(dve_free, 1)
                    elif s in (12, 13):
                        c = 2 * (s - 12)
                        dve.wait_ge(act_free, unit_count(NU - 1, "act") * l + unit_count(U_CONV_C + s - 12, "act"))
                        v.tensor_tensor(bufB[:, c:c + 2, 2:T + 2], pa(s - 4), bufA[:, c:c + 2],
                                        ALU.mult).then_inc(dve_free, 1)
                        if s == 13:
                            dve.wait_ge(dve_free, unit_count(NU - 1, "dve") * l + unit_count(U_CONV_H + 1, "dve"))
                            for k in (2, 1, 0):
                                conv(k)
                    elif s in (14, 15):
                        c = 2 * (s - 14)
                        ins = v.tensor_tensor(bufC[:, c:c + 2], bufC[:, c:c + 2], pa(s - 4), ALU.mult)
                        ins.then_inc(dve_free, 1)
                        if s == 15:
                            dve.wait_ge(yB_hi, l + 1)
                            v.tensor_tensor(act_lo[:, 0:4], bufC[:, :, :], act_hi[:, 0:4],
                                            ALU.subtract).then_inc(yB_lo, 1)
                    elif s in (16, 17):
                        rotary(rqT[:, 2 * (s - 16):2 * (s - 16) + 2], s - 4)
                    elif s in (18, 19):
                        rotary(rkT[:, 2 * (s - 18):2 * (s - 18) + 2], s - 4)
                    elif BRANCH0 <= s < OUT0:
                        b, n = divmod(s - BRANCH0, 6)
                        if n not in (2, 5):
                            return
                        half = n // 5
                        for m in range(2):
                            u = U_BR + 8 * b + 2 + 4 * half + m
                            if m == 0:
                                dve.wait_ge(half_unit, 6 * l + 2 * b + half + 1)
                            else:
                                dve.wait_ge(sub_used, base + s + 1)
                            dve.wait_ge(act_free, unit_count(NU - 1, "act") * l + unit_count(u - 2, "act"))
                            gated(u, b, 4 * half + 2 * m)
                        if b == LAST_BRANCH:
                            for m in range(2):
                                c = 4 * half + 2 * m
                                q = (c + 4) % DK
                                dve.wait_ge(m_hi, 4 * l + 2 * half + m + 1)
                                v.scalar_tensor_tensor(act_lo[:, q:q + 2], merged[:, c:c + 2], 0.5,
                                                       act_hi[:, q:q + 2], ALU.mult, ALU.subtract).then_inc(m_lo, 1)

                def maxima(j):
                    kind, qt, g, a = STEPS[j]
                    dve.wait_ge(s_ps, NS * l + j + 1)
                    if kind == "cmp":
                        s = PS[:, SB:SB + 2, 0:8 * NH].rearrange("p b (i n) -> p b i n", n=16)[:, :, :, 0:NC]
                        dve.wait_ge(pt_ps, NS * l + j)
                        top = stat[:, 0:NH].rearrange("p (b i) -> p b i", b=2)
                        chain.link(v.reduce_max(top, s, AX_X))
                        v.tensor_tensor(cprob[:, :, :].rearrange("p (b i) n -> p b i n", b=2), s,
                                        top.unsqueeze(3).broadcast_to([P, 2, NH // 2, NC]),
                                        ALU.subtract).then_inc(max_rdy, 1)
                        return
                    w = (qt + 1) * P
                    s = PS[:, SB:SB + 2, :].rearrange("p b (r k) -> p (b r) k", r=2)[:, :, 0:w]
                    chain.link(v.reduce_max(stat[:, 0:NR], s, AX_X))
                    v.tensor_scalar(stat[:, 8:8 + NR], stat[:, 0:NR], -DH ** -0.5, None,
                                    ALU.mult).then_inc(max_rdy, 1)

                def normalise(j):
                    kind, qt, g, a = STEPS[j]
                    dve.wait_ge(exp_rdy, NS * l + j + 1)
                    if j == 0:
                        dve.wait_ge(v_rdy, l + 1)
                    gates = gate[:, qt, :].rearrange("p (i par a) -> p par i a", par=2, a=3)
                    if kind == "cmp":
                        w = valid[:, qt, :].unsqueeze(1).broadcast_to([P, NH, NC])
                        chain.link(v.tensor_tensor(cprob[:, :, :], cprob[:, :, :], w, ALU.mult))
                        chain.link(v.reduce_sum(stat[:, 24:24 + NH], cprob[:, :, :], AX_X))
                        chain.link(v.tensor_scalar(stat[:, 24:24 + NH], stat[:, 24:24 + NH], 1e-30, None, ALU.max))
                        chain.link(v.reciprocal(stat[:, 32:32 + NH], stat[:, 24:24 + NH]))
                        chain.link(v.tensor_tensor(stat[:, 40:40 + NH].rearrange("p (b i) -> p b i", b=2),
                                                   stat[:, 32:32 + NH].rearrange("p (b i) -> p b i", b=2),
                                                   gates[:, :, :, 0], ALU.mult))
                        v.tensor_tensor(cprob[:, :, :], cprob[:, :, :],
                                        stat[:, 40:40 + NH].unsqueeze(2).broadcast_to([P, NH, NC]),
                                        ALU.mult).then_inc(prob_rdy, 1)
                        return
                    w = (qt + 1) * P
                    chain.link(v.reciprocal(stat[:, 32:32 + NR], stat[:, 16:16 + NR]))
                    chain.link(v.tensor_tensor(stat[:, 40:40 + NR].rearrange("p (b i) -> p b i", b=2),
                                               stat[:, 32:32 + NR].rearrange("p (b i) -> p b i", b=2),
                                               gates[:, :, 2 * g:2 * g + 2, 1 + a], ALU.mult))
                    v.tensor_tensor(prob[:, :, 0:w], prob[:, :, 0:w],
                                    stat[:, 40:40 + NR].unsqueeze(2).broadcast_to([P, NR, w]),
                                    ALU.mult).then_inc(prob_rdy, 1)

                def drain_transposes(j):
                    kind, qt, g, a = STEPS[j]
                    if kind != "cmp" and qt == 0:
                        return
                    dve.wait_ge(pt_ps, NS * l + j + 1)
                    if kind == "cmp":
                        v.tensor_copy(cprobT[0:NC, 512:1024], PS[0:NC, TB + 1, :]).then_inc(ptD_rdy, 1)
                    else:
                        v.tensor_copy(probT[:, 512:1024], PS[:, TB + 1, :]).then_inc(ptD_rdy, 1)

                def drain_group(j):
                    kind, qt, g, a = STEPS[j]
                    dve.wait_ge(yA_hi, len(GROUP_ENDS) * l + GROUP_ENDS.index(j) + 1)
                    at = (slice(None), slice(4 + 2 * g, 6 + 2 * g), slice(qt * P, (qt + 1) * P))
                    v.tensor_tensor(act_lo[at], PS[:, YB, 0:2 * P].rearrange("p (c t) -> p c t", c=2), act_hi[at],
                                    ALU.subtract).then_inc(yA_lo, 1)

                def decayed(h):
                    dve.wait_ge(rs_ps, RH * l + h + 1)
                    b = h % 2
                    if h >= 2:
                        dve.wait_ge(ra_ps, RH * l + h - 1)
                    v.tensor_tensor(inn[:, b, 0:T], PS[:, SB + b, 0:T], decay[:, h, :], ALU.mult)
                    v.tensor_tensor(inn[:, b, T:T + P], PS[:, SB + b, T:T + P], decay[:, h, 0:P],
                                    ALU.mult).then_inc(inn_rdy, 1)

                def group_norm():
                    dve.wait_ge(ra_ps, RH * (l + 1))
                    o = [PS[:, TB + n // RH, (n % RH) * P:(n % RH + 1) * P] for n in range(8)]
                    for n in range(8):
                        last = v.bn_stats(bst[:, n, :], o[n])
                    chain.link(last)
                    for n in range(8):
                        last = v.bn_aggr(mv[:, n, :], bst[:, n, :])
                    last.then_inc(gvar_rdy, 1)
                    dve.wait_ge(gstd_rdy, l + 1)
                    chain.link(v.reciprocal(rstd[:, 0:8], rstd[:, 0:8]))
                    for n in range(8):
                        last = v.tensor_scalar(onorm[:, n // RH, (n % RH) * P:(n % RH + 1) * P], o[n], mv[:, n, 0:1],
                                               rstd[:, n:n + 1], ALU.subtract, ALU.mult)
                    last.then_inc(on_rdy, 1)

                def retained():
                    dve.wait_ge(rt_ps, l + 1)
                    for h in range(RH):
                        last = v.tensor_scalar(bufC[:, h, :], PS[:, SB + h // 2, (h % 2) * T:(h % 2 + 1) * T],
                                               sm[:, l, S_GNG + h:S_GNG + h + 1], sm[:, l, S_GNB + h:S_GNB + h + 1],
                                               ALU.mult, ALU.add)
                    chain.link(last)
                    v.scalar_tensor_tensor(bufC[:, :, :], bufC[:, :, :], 0.5, rkT, ALU.mult,
                                           ALU.mult).then_inc(yC_rdy, 1)

                def retained_lower():
                    dve.wait_ge(yC_hi, l + 1)
                    v.tensor_tensor(act_lo[:, 0:4], bufC[:, :, :], act_hi[:, 0:4], ALU.subtract).then_inc(yC_lo, 1)

                for s in range(MIX):
                    after(s)
                    if s == 8:
                        dve.wait_ge(ht_ps, l + 1)
                        for kv in range(2):
                            o = PS[:, MB, 2 * ZM * kv:2 * ZM * (kv + 1)].rearrange("p (c n) -> p c n", c=2)
                            last = v.tensor_tensor(hbias[:, 2 * kv:2 * kv + 2], o[:, :, 32 * (kv + 1)],
                                                   sm[:, l, S_B1 + 2 * kv:S_B1 + 2 * kv + 2], ALU.add)
                        last.then_inc(hbias_rdy, 1)
                    if s == 9:
                        dve.wait_ge(w2_ps, l + 1)
                        v.tensor_scalar(kcT[:, :, :].rearrange("p g n -> p (g n)"), PS[:, MB, 0:NG * NC],
                                        sm[:, l, S_B2K:S_B2K + 1], None, ALU.add)
                        v.tensor_copy(Vc[:, :, :].rearrange("p g c -> p (g c)"),
                                      PS[0:NC, MB, 64:64 + NG * DH]).then_inc(kc_rdy, 1)
                    j, late = divmod(s + 1 - STEP0, 2)
                    if 0 <= j < NS and not late:
                        maxima(j)
                    if s == RET0 + 3:
                        retained()
                    if s < MIX - 2:
                        split(base + s + RING)
                    if 0 <= j <= NS:
                        if late:
                            if j - 1 in GROUP_ENDS:
                                drain_group(j - 1)
                            if j < NS:
                                drain_transposes(j)
                        elif j < NS:
                            normalise(j)
                    if s == RET0 - 1:
                        decayed(0)
                        decayed(1)
                    if s == RET0:
                        decayed(2)
                        decayed(3)
                    if s == RET0 + 1:
                        group_norm()
                    if s == RET0 + 2:
                        dve.wait_ge(tanh_rdy, l + 1)
                        chain.link(v.scalar_tensor_tensor(rkT, rkT, 1.0, rg[:, :, :], ALU.add, ALU.mult))
                    if s == RET0 + 3:
                        retained_lower()

            def dense():
                f0 = MIX

                def hidden_half(b, s, n):
                    dve.wait_ge(sub_used, s + 1)
                    dve.wait_ge(silu_rdy, b * 2 + (n + 1))
                    v.tensor_tensor(hidden[:, 2 * n:2 * n + 2], PS[:, 6 + n, :].rearrange("p (c t) -> p c t", c=2),
                                    silu[:, 2 * n:2 * n + 2], ALU.mult).then_inc(hid_ff, 1)
                    dve.wait_ge(hT_hi_rdy, b * 2 + (n + 1))
                    v.tensor_tensor(act_lo[:, 2 * n:2 * n + 2], hidden[:, 2 * n:2 * n + 2], act_hi[:, 2 * n:2 * n + 2],
                                    ALU.subtract).then_inc(hT_rdy, 1)

                def body(b, k, at):
                    for c in range(6):
                        if c < 2:
                            hidden_half(b, k * 6 + (at + c), c)
                        split(at + c + RING, k)

                split(f0 + RING)
                split(f0 + 1 + RING)
                body(0, 0, f0 + 2)
                with dve.Fori(1, NB - 1) as b:
                    body(b, b - 1, f0 + 8)
                for c in range(2):
                    hidden_half(NB - 1, f0 + FFN - 4 + c, c)
                    split(f0 + FFN - 4 + c + RING)

            def routing():
                def at(a, n, k):
                    return route[:, a:a + n * k].rearrange("p (n k) -> p n k", n=n)
                lg, mx, ix, m1, m2, ch = (at(16 * n, TT, NE) for n in range(6))
                link = chain.link
                v.tensor_scalar(acc, X[:, :, :], ALPHA, None, ALU.mult).then_inc(acc_rdy, 1)
                link(v.memset(items[:, :, NI, :], -1.0))
                dve.wait_ge(log2_ps, 1)
                link(v.tensor_copy(lg, PS[:, 1, 0:TT * NE].rearrange("p (n k) -> p n k", n=TT)))
                for t in range(TT):
                    last = v.max(mx[:, t, :], lg[:, t, :])
                link(last)
                for t in range(TT):
                    last = v.max_index(idx8[:, t, :], mx[:, t, :], lg[:, t, :])
                link(last)
                link(v.tensor_copy(ix, idx8[:, :, :]))
                io = iota8.unsqueeze(1).broadcast_to([P, TT, NE])

                def wide(a):
                    return a.broadcast_to([P, TT, NE])
                v.tensor_tensor(m1, io, wide(ix[:, :, 0:1]), ALU.is_equal)
                link(v.tensor_tensor(m2, io, wide(ix[:, :, 1:2]), ALU.is_equal))
                v.tensor_tensor(chosen_b[:, :, :], m1, m2, ALU.add).then_inc(cnt_in, 1)
                v.tensor_tensor(ch, m1, m2, ALU.add)
                v.tensor_tensor(route[:, 98:100], mx[:, :, 1], mx[:, :, 0], ALU.subtract).then_inc(router_exp, 1)
                dve.wait_ge(router_exped, 1)
                e, s, p1, p2 = (route[:, a:a + 2] for a in (96, 100, 102, 104))
                link(v.tensor_scalar(s, e, 1.0, None, ALU.add))
                link(v.reciprocal(p1, s))
                link(v.tensor_tensor(p2, e, p1, ALU.mult))
                w1, w2 = at(112, TT, NE), at(128, TT, NE)
                v.tensor_tensor(w1, m1, wide(p1.unsqueeze(2)), ALU.mult)
                link(v.tensor_tensor(w2, m2, wide(p2.unsqueeze(2)), ALU.mult))
                pos, wgt = items[:, :, 0:NE, 0], items[:, :, 0:NE, 1]
                v.tensor_tensor(wgt, w1, w2, ALU.add)
                dve.wait_ge(cnt_ps, 1)
                po = at(144, TT, NE)
                link(v.scalar_tensor_tensor(po, PS[:, 0, 0:TT * NE].rearrange("p (n k) -> p n k", n=TT), 1.0, ch,
                                            ALU.add, ALU.mult))
                link(v.tensor_scalar(pos, po, -1.0, None, ALU.add))
                picks(0)
                over, rank, pr = route[:, 160:168], route[:, 168:176], at(192, NE, NE)
                sel, named = at(256, NX, NE), at(256 + NX * NE, NX, NE)
                link(v.tensor_scalar(over, PS[:, 0, 2 * NE:3 * NE], float(P), None, ALU.is_gt))
                link(v.tensor_tensor(pr, tri8, over.unsqueeze(1).broadcast_to([P, NE, NE]), ALU.mult))
                v.reduce_sum(rank, pr, AX_X)
                count = route[:, 184:185]
                link(v.reduce_sum(count, over, AX_X))
                past = at(144, TT, NE)
                v.tensor_scalar(past, pos, float(1 - P), None, ALU.add)
                link(v.tensor_tensor(sel, rank.unsqueeze(1).broadcast_to([P, NX, NE]),
                                     iota8[:, 0:NX].unsqueeze(2).broadcast_to([P, NX, NE]), ALU.is_equal))
                link(v.tensor_tensor(sel, sel, over.unsqueeze(1).broadcast_to([P, NX, NE]), ALU.mult))
                chosen = [at(320 + TT * NX * NE * n, TT * NX, NE).rearrange("p (t j) e -> p t j e", t=TT)
                          for n in range(2)]
                v.tensor_tensor(named, sel, iota8.unsqueeze(1).broadcast_to([P, NX, NE]), ALU.mult)
                for t in range(TT):
                    for n, of in enumerate((past, wgt)):
                        last = v.tensor_tensor(chosen[n][:, t], sel, of[:, t, :].unsqueeze(1).broadcast_to([P, NX, NE]),
                                               ALU.mult)
                link(last)
                number = route[:, 186:186 + NX]
                v.reduce_sum(number, named, AX_X)
                for t in range(TT):
                    v.reduce_sum(items[:, t, NE:NI, 0], chosen[0][:, t], AX_X)
                    last = v.reduce_sum(items[:, t, NE:NI, 1], chosen[1][:, t], AX_X)
                link(last)
                v.tensor_scalar(items[:, :, NE:NI, 0], items[:, :, NE:NI, 0], -1.0, None, ALU.add)
                v.tensor_copy(table[0:1, 0:NX], number[0:1, :])
                v.tensor_copy(table[0:1, NX:NX + 1], count[0:1, :])
                v.tensor_scalar(table[0:1, NX + 1:NX + 2], count[0:1, :], float(NE), None,
                                ALU.add).then_inc(table_rdy, 1)
                dve.wait_ge(table_rdy, 1)
                gather(0)

            def picks(i):
                for t in range(TT):
                    last = v.tensor_scalar(pick[:, t, :], iota, items[:, t, bass.ds(i, 1), 0], None, ALU.is_equal)
                last.then_inc(pick_rdy, 1)

            def gather(i):
                for c in range(2):
                    dve.wait_ge(xe_hi_rdy, i * 2 + (c + 1))
                    v.tensor_tensor(xe_lo[:, 4 * c:4 * c + 4, :], PS[:, TB + c, :].rearrange("p (k t) -> p k t", k=4),
                                    xe_hi[:, 4 * c:4 * c + 4, :], ALU.subtract).then_inc(xe_rdy, 1)

            def experts():
                n_items = dve.value_load(table[0:1, NX + 1:NX + 2], min_val=NE, max_val=NI)

                def hidden_block(n, s):
                    dve.wait_ge(sub_used, s + 1)
                    dve.wait_ge(esilu_rdy, n + 1)
                    v.tensor_tensor(hidden_e, PS[:, 1, :], silu_e, ALU.mult).then_inc(ehid_rdy, 1)

                def lower(n):
                    dve.wait_ge(ehT_hi, n + 1)
                    v.tensor_tensor(hT_lo, PS[:, YB, :], hT_hi, ALU.subtract).then_inc(ehT_rdy, 1)

                def body(n, k, s):
                    for c in range(6):
                        if c == 1:
                            hidden_block(n, s + 1)
                        if c == 2:
                            lower(n)
                        split(MOE0 + 2 + c + RING, k)

                def add_scattered(i):
                    for n in range(4):
                        t, c = divmod(n, 2)
                        dve.wait_ge(scat_ps, i * 4 + (n + 1))
                        o = acc[:, t, c * 512:(c + 1) * 512]
                        if n == 0:
                            dve.wait_ge(acc_rdy, i * 4 + 1)
                        v.tensor_tensor(o, o, PS[:, SCATTER[n], :], ALU.add).then_inc(acc_rdy, 1)

                with dve.Fori(0, n_items) as i:
                    s0 = i * FFN + MOE0
                    for t in range(TT):
                        last = v.tensor_scalar(pickw[:, t, :], iota, items[:, t, bass.ds(i, 1), 0],
                                               items[:, t, bass.ds(i, 1), 1], ALU.is_equal, ALU.mult)
                    last.then_inc(pickw_rdy, 1)
                    dve.wait_ge(gather_ps, i * 2 + 2)
                    picks(i + 1)
                    split(MOE0 + RING, i * NB)
                    split(MOE0 + 1 + RING, i * NB)
                    add_scattered(i)
                    body(i * NB, i * NB, s0 + 2)
                    with dve.Fori(1, NB - 1) as b:
                        body(i * NB + b, i * NB + b, s0 + b * 6 + 2)
                    k = i * NB + (NB - 1)
                    split(MOE0 + 2 + RING, k)
                    hidden_block(k, s0 + (FFN - 3))
                    split(MOE0 + 3 + RING, k)
                    lower(k)
                    gather(i + 1)
                    split(MOE0 + 4 + RING, k)
                    split(MOE0 + 5 + RING, k)
                add_scattered(n_items)
                dve.wait_ge(acc_rdy, n_items * 4 + 5)

            v.memset(bufB[:, :, 0:2], 0.0)
            v.memset(eps[:, :], EPS).then_inc(const_rdy, 1)
            norm(0)
            split(0)
            split(1)
            dve.wait_ge(const_in, 16 * 3)
            v.tensor_copy(cb[:, :], cstf).then_inc(const_rdy, 1)
            split(2)
            mixer(0)
            norm(1)
            dense()
            norm(2)
            mixer(1)
            norm(3)
            routing()
            experts()
            norm(4)


def host_layout(a):
    def rows(w, k):
        return w.reshape(k, P, -1).transpose(1, 0, 2)

    def cut(w, k):
        w = rows(w, k)
        n = w.shape[2] // 256
        return w.reshape(P, k, n, 256).transpose(2, 0, 1, 3).reshape(n, P, SUB)

    subs = []
    for l in range(L):
        w = a["w_in"][l]
        q, kv, ng, rest = w[:, :512], w[:, 512:1280], w[:, 1280:1304], w[:, 1304:]
        ngp = np.zeros((D, 256), np.float32)
        ngp[:, :24] = ng
        conv_b, conv_c, conv_h = rest[:, :512], rest[:, 512:1024], rest[:, 1024:1536]
        ret, mg = rest[:, 1536:3584], rest[:, 3584:].reshape(D, 3, D)
        first = list(cut(np.concatenate([q, kv, ngp], 1), DK))
        subs += first[:4]
        for kv_ in range(2):
            w1 = a["cmp_w1"][l, kv_].reshape(16, P, CH)
            for h in range(2):
                subs.append(w1[8 * h:8 * h + 8].transpose(1, 0, 2).reshape(P, SUB))
        subs += first[4:]
        subs += list(cut(np.concatenate([conv_c, conv_h, conv_b, ret], 1), DK))
        for b in (1, 0, 2):
            g = cut(mg[:, b], DK)
            br = [rows(a["w_br"][l, b][:, c * 512:(c + 1) * 512], 4).reshape(P, SUB) for c in range(2)]
            subs += [g[0], g[1], br[0], g[2], g[3], br[1]]
        for c in range(2):
            wo = rows(a["w_out"][l][:, c * 512:(c + 1) * 512], DK)
            subs += [wo[:, 4 * h:4 * h + 4].reshape(P, SUB) for h in range(2)]
        if l == 0:
            gate, up, down = a["ffn_gate"][0], a["ffn_up"][0], a["ffn_down"][0]
            g, u = cut(gate, DK), cut(up, DK)
            d = down.reshape(2 * NB, 2, P, D).transpose(0, 2, 1, 3).reshape(2 * NB, P, SUB)
            subs += [g[0], g[1]]
            for b in range(NB):
                subs += [u[2 * b], u[2 * b + 1]]
                if b + 1 < NB:
                    subs += [g[2 * b + 2], g[2 * b + 3]]
                subs += [d[2 * b], d[2 * b + 1]]
    head = np.stack(subs).reshape(-1, 2, P, SUB).transpose(0, 2, 1, 3).reshape(-1, P, 2 * SUB)
    stream = np.empty((NTILES, P, 2 * SUB), np.float32)
    stream[:len(head)] = head
    assert len(head) == MOE0 // 2
    t = len(head)

    def wide(w):
        return rows(w, DK).reshape(P, DK, NB, 512).transpose(2, 0, 1, 3).reshape(NB, P, 2 * SUB)
    for e in range(NE):
        g, u = wide(a["moe_gate"][0, e]), wide(a["moe_up"][0, e])
        d = a["moe_down"][0, e].reshape(NB, 4, P, D).transpose(0, 2, 1, 3).reshape(NB, P, 2 * SUB)
        stream[t] = g[0]
        t += 1
        for b in range(NB):
            stream[t] = u[b]
            t += 1
            if b + 1 < NB:
                stream[t] = g[b + 1]
                t += 1
            stream[t] = d[b]
            t += 1
    assert t == NTILES

    small = np.zeros((L, P, S_W), np.float32)
    for l in range(L):
        s = small[l]
        for kv in range(2):
            s[:, S_POS + kv * P:S_POS + kv * P + 16] = a["cmp_pos"][l, kv].reshape(16, P).T
        s[:, S_B1:S_B1 + 4] = a["cmp_b1"][l].reshape(4, P).T
        w2 = a["cmp_w2"][l].reshape(2, 2, P, DH)
        for c in range(2):
            s[:, S_W2K + c * P:S_W2K + c * P + DH] = w2[0, c]
            s[:, S_W2K + c * P + DH:S_W2K + (c + 1) * P] = w2[0, c]
            s[:, S_W2V + c * DH:S_W2V + (c + 1) * DH] = w2[1, c]
        s[:DH, S_B2K] = a["cmp_b2"][l, 0]
        s[DH:, S_B2K] = a["cmp_b2"][l, 0]
        s[:, S_CONV:S_CONV + 12] = a["conv_w"][l].reshape(12, P).T
        s[:, S_GNG:S_GNG + 4] = a["ret_gn_g"][l].reshape(4, P).T
        s[:, S_GNB:S_GNB + 4] = a["ret_gn_b"][l].reshape(4, P).T
        s[0, S_B2V:S_B2V + DH] = a["cmp_b2"][l, 1]
    ln = np.stack([np.stack([a[f"ln{n}_g"][l], a[f"ln{n}_b"][l]]) for l in range(L) for n in (1, 2)])
    router = np.zeros((P, DK, P), np.float32)
    router[:, :, :NE] = rows(a["moe_router"][0], DK)
    return stream, small, ln, router


def constants():
    c = np.zeros((P, C_W), np.float32)
    c[:, C_ID:C_ID + P] = np.eye(P)
    i = np.arange(P, dtype=np.float64)
    for h in range(RH):
        log_g = np.log(1.0 - 2.0 ** (-5.0 - h))
        d = i[None, :] - i[:, None]
        at = C_DEC + 256 * h
        c[:, at:at + P] = np.where(d >= 0, np.exp(log_g * np.maximum(d, 0)), 0) * RD ** -0.5
        c[:, at + P:at + 2 * P] = np.exp(log_g * (d + P)) * RD ** -0.5
    inv = (10000.0 ** (-np.arange(0, RD, 2, dtype=np.float32) / RD)).astype(np.float32)
    ang = inv[:, None] * np.arange(T, dtype=np.float32)[None, :]
    c[:, C_COS:C_COS + T] = np.tile(np.cos(ang), (2, 1))
    c[:, C_SIN:C_SIN + T] = np.concatenate([np.sin(ang), -np.sin(ang)])
    c[:, C_IOTA:C_IOTA + P] = i
    c[:, C_IOTA8:C_IOTA8 + NE] = np.arange(NE)
    c[:, C_TRI8:C_TRI8 + NE * NE] = np.tril(np.ones((NE, NE)), -1).reshape(-1)
    q = np.arange(T).reshape(TT, P).T
    ok = q[:, :, None] >= (np.arange(NC) * CS + CL - 1)[None, None, :]
    c[:, C_VALID:C_VALID + TT * NC] = ok.reshape(P, -1)
    c[:, C_ONES:C_ONES + NC] = 1
    b = np.zeros((P, B_W), np.float32)
    b[:, B_ID:B_ID + P] = np.eye(P)
    b[:, B_MASK + P:B_MASK + 2 * P] = np.where(i[None, :] <= i[:, None], 0, NEG)
    b[:, B_CMP:B_CMP + TT * NC] = np.where(ok, 0, NEG).reshape(P, -1)
    b[:, B_LT:B_LT + P] = i[:, None] < i[None, :]
    b[:, B_ONE:B_ONE + P] = 1
    return c, b


def kernel(**inputs):
    import concourse.bacc as bacc
    from concourse.bass_utils import run_bass_kernel_spmd

    a = {k: np.asarray(v) for k, v in inputs.items()}
    stream, small, ln, router = host_layout(a)
    consts, constb = constants()
    nc = bacc.Bacc("TRN2", target_bir_lowering=False, num_devices=1,
                   dynamic_dma_scratch_size=4096)
    arrays = {"wstream": stream, "x": np.ascontiguousarray(a["x"].reshape(T, D)), "consts": consts, "constb": constb,
              "small": small, "ln": ln, "router": router}
    aps = [nc.dram_tensor(n, v.shape, F32, kind="ExternalInput").ap() for n, v in arrays.items()]
    out = nc.dram_tensor("out", (T, D), F32, kind="ExternalOutput").ap()
    trunk(nc, *aps, out)
    r = run_bass_kernel_spmd(nc, [arrays], core_ids=[0])
    return r.results[0]["out"].reshape(1, T, D)
```
